# Optimizing a Trainium2 kernel written in Bass

```python
import math
import jax, jax.numpy as jnp
from jax import lax
import numpy as np

D_MODEL = 2048
BATCH = 1
SEQ = 256
DEPTH = 1

N_META = 16
MIX_WIDTH = D_MODEL
POOL_WIDTH = MIX_WIDTH // 2
CONV_WIDTH = MIX_WIDTH - POOL_WIDTH
POOL_WINDOWS = (2, 4, 8, 16)
N_POOL_GROUPS = len(POOL_WINDOWS)
POOL_GROUP_DIM = POOL_WIDTH // N_POOL_GROUPS
CONV_HEADS = 8
CONV_KSIZE = 31
IN_WIDTH = POOL_WIDTH + 2 * CONV_WIDTH
PEER_HEADS = 8
PEER_NKEYS = 128
PEER_EXPERTS = PEER_NKEYS * PEER_NKEYS
PEER_QDIM = 256
PEER_HALF = PEER_QDIM // 2
PEER_TOPK = 16
PEER_ROWS = 16
RMS_EPS = 1e-6
LN_EPS = 1e-5

kernel_name = "hymba_pool_conformer_peer_block"

def rms_norm(x, g):
    xf = x.astype(jnp.float32)
    y = xf * lax.rsqrt(jnp.mean(xf * xf, axis=-1, keepdims=True) + RMS_EPS)
    return (y * g.astype(jnp.float32)).astype(x.dtype)

def layer_norm(x, g, b):
    xf = x.astype(jnp.float32)
    mu = jnp.mean(xf, axis=-1, keepdims=True)
    xc = xf - mu
    var = jnp.mean(xc * xc, axis=-1, keepdims=True)
    y = xc * lax.rsqrt(var + LN_EPS) * g.astype(jnp.float32) + b.astype(jnp.float32)
    return y.astype(x.dtype)

def causal_multiscale_pool(xp):
    T = xp.shape[1]
    xf = xp.astype(jnp.float32)
    c0 = jnp.concatenate([jnp.zeros_like(xf[:, :1]), jnp.cumsum(xf, axis=1)], axis=1)
    t = jnp.arange(T, dtype=jnp.int32)
    win = jnp.array(POOL_WINDOWS, dtype=jnp.int32)
    lo = jnp.maximum(t[:, None] + 1 - win[None, :], 0)
    g_idx = jnp.arange(N_POOL_GROUPS, dtype=jnp.int32)[None, :]
    window_sum = c0[:, 1:] - c0[:, lo, g_idx]
    count = (t[:, None] + 1 - lo).astype(jnp.float32)
    mean = window_sum / count[None, :, :, None]
    return (mean - xf).astype(xp.dtype)

def causal_depthwise_conv(x, w, b):
    C = x.shape[-1]
    K = w.shape[0]
    y = lax.conv_general_dilated(
        x, w[:, None, :], window_strides=(1,), padding=[(K - 1, 0)],
        dimension_numbers=("NWC", "WIO", "NWC"), feature_group_count=C)
    return y + b

def peer_ffn(xn, wq, keys, down, up):
    B, T, D = xn.shape
    q = (xn @ wq).reshape(B, T, PEER_HEADS, 2, PEER_HALF)
    s = jnp.einsum("bthpd,hpnd->bthpn", q, keys).astype(jnp.float32)
    sv, si = lax.top_k(s, PEER_TOPK)
    cand_score = (sv[..., 0, :, None] + sv[..., 1, None, :]).reshape(B, T, PEER_HEADS, PEER_TOPK * PEER_TOPK)
    cand_idx = (si[..., 0, :, None] * PEER_NKEYS + si[..., 1, None, :]).reshape(B, T, PEER_HEADS, PEER_TOPK * PEER_TOPK)
    top_score, pos = lax.top_k(cand_score, PEER_TOPK)
    expert_idx = jnp.take_along_axis(cand_idx, pos, axis=-1)
    gate = jax.nn.softmax(top_score, axis=-1).astype(xn.dtype)

    R = B * T
    nb = R // PEER_ROWS

    def block(args):
        xb, ib, gb = args
        u = jnp.take(down, ib, axis=0)
        hidden = jnp.einsum("rd,rhkd->rhk", xb, u)
        act = gb * jax.nn.gelu(hidden, approximate=False)
        v = jnp.take(up, ib, axis=0)
        return jnp.einsum("rhk,rhkd->rd", act, v)

    out = lax.map(block, (xn.reshape(nb, PEER_ROWS, D),
                          expert_idx.reshape(nb, PEER_ROWS, PEER_HEADS, PEER_TOPK),
                          gate.reshape(nb, PEER_ROWS, PEER_HEADS, PEER_TOPK)))
    return out.reshape(B, T, D)

def setup_inputs(seed: int = 0) -> dict:
    key = jax.random.key(seed)
    ks = jax.random.split(key, 20)
    f32 = jnp.float32
    D, L = D_MODEL, DEPTH

    def nrm(k, shape, scale):
        return jax.random.normal(k, shape, f32) * scale

    return {
        "x": nrm(ks[0], (BATCH, SEQ, D), 1.0),
        "meta_tokens": nrm(ks[1], (N_META, D), 1.0),
        "mix_norm_g": 1.0 + nrm(ks[2], (L, D), 0.02),
        "w_in": nrm(ks[3], (L, D, IN_WIDTH), D ** -0.5),
        "pool_w": nrm(ks[4], (L, N_POOL_GROUPS, POOL_GROUP_DIM, POOL_GROUP_DIM), POOL_GROUP_DIM ** -0.5),
        "pool_scale": 1.0 + nrm(ks[5], (L, POOL_WIDTH), 0.02),
        "conv_dw_w": nrm(ks[6], (L, CONV_KSIZE, CONV_WIDTH), CONV_KSIZE ** -0.5),
        "conv_dw_b": nrm(ks[7], (L, CONV_WIDTH), 0.02),
        "conv_ln_g": 1.0 + nrm(ks[8], (L, CONV_WIDTH), 0.02),
        "conv_ln_b": nrm(ks[9], (L, CONV_WIDTH), 0.02),
        "conv_pw_w": nrm(ks[10], (L, CONV_WIDTH, CONV_WIDTH), CONV_WIDTH ** -0.5),
        "conv_pw_b": nrm(ks[11], (L, CONV_WIDTH), 0.02),
        "w_out": nrm(ks[12], (L, MIX_WIDTH, D), MIX_WIDTH ** -0.5),
        "ffn_norm_g": 1.0 + nrm(ks[13], (L, D), 0.02),
        "peer_wq": nrm(ks[14], (L, D, PEER_HEADS * PEER_QDIM), D ** -0.5),
        "peer_keys": nrm(ks[15], (L, PEER_HEADS, 2, PEER_NKEYS, PEER_HALF), PEER_HALF ** -0.5),
        "peer_down": nrm(ks[16], (L, PEER_EXPERTS, D), D ** -0.5),
        "peer_up": nrm(ks[17], (L, PEER_EXPERTS, D), 0.5),
        "final_norm_g": 1.0 + nrm(ks[18], (D,), 0.02),
    }

def reference(x, meta_tokens, mix_norm_g, w_in, pool_w, pool_scale, conv_dw_w, conv_dw_b,
              conv_ln_g, conv_ln_b, conv_pw_w, conv_pw_b, w_out, ffn_norm_g, peer_wq,
              peer_keys, peer_down, peer_up, final_norm_g):
    B = x.shape[0]
    meta = jnp.broadcast_to(meta_tokens[None].astype(x.dtype), (B, N_META, D_MODEL))
    h = jnp.concatenate([meta, x], axis=1)
    T = h.shape[1]
    for l in range(DEPTH):
        hn = rms_norm(h, mix_norm_g[l])
        proj = hn @ w_in[l]
        xp = proj[..., :POOL_WIDTH]
        xa = proj[..., POOL_WIDTH:POOL_WIDTH + CONV_WIDTH]
        xg = proj[..., POOL_WIDTH + CONV_WIDTH:]
        pooled = causal_multiscale_pool(xp.reshape(B, T, N_POOL_GROUPS, POOL_GROUP_DIM))
        ya = jnp.einsum("btgc,gcd->btgd", pooled, pool_w[l]).reshape(B, T, POOL_WIDTH) * pool_scale[l]
        glu = xa * jax.nn.sigmoid(xg)
        cv = causal_depthwise_conv(glu, conv_dw_w[l], conv_dw_b[l])
        cv = jax.nn.silu(layer_norm(cv, conv_ln_g[l], conv_ln_b[l]))
        yb = cv @ conv_pw_w[l] + conv_pw_b[l]
        h = h + jnp.concatenate([ya, yb], axis=-1) @ w_out[l]
        h = h + peer_ffn(rms_norm(h, ffn_norm_g[l]), peer_wq[l], peer_keys[l], peer_down[l], peer_up[l])
    h = rms_norm(h, final_norm_g)
    return h[:, N_META:]


_drawn_inputs = setup_inputs


def setup_inputs(seed=0):
    import zlib

    import numpy as np

    out = dict(_drawn_inputs(seed))
    spreads = {}
    factors = {}
    for name, (base, spread) in spreads.items():
        noise = np.random.default_rng([zlib.crc32(name.encode()), seed]).standard_normal(out[name].shape)
        drawn = base * np.exp(spread * noise) if base else spread * noise
        out[name] = __import__('jax').numpy.asarray(drawn.astype(out[name].dtype))
    for name, factor in factors.items():
        out[name] = (out[name] * factor).astype(out[name].dtype)
    return out
```

```python
from contextlib import ExitStack

import concourse.bass as bass
from concourse import mybir

P = 128
F32 = mybir.dt.float32
F32R = mybir.dt.float32r
U32 = mybir.dt.uint32
ALU = mybir.AluOpType
ACT = mybir.ActivationFunctionType
AX = mybir.AxisListType

D = 2048
KD = D // P
META, SEQ = 16, 256
T = META + SEQ
TT = SEQ // P
W = 1024
CT = W // P
TAPS = 31
PAD = TAPS - 1 - META
WINDOWS = (2, 4, 8, 16)
HEADS, TOPK, NKEYS = 8, 16, 128
SLOTS = HEADS * TOPK
RMS_EPS, LN_EPS = 1e-6, 1e-5
LOWEST = -3.4028235e38

CHUNK = 1024
PROJ_TILES = 3 * CT
C_PROJ = 2 * PROJ_TILES
C_PW = CT
C_POOL = 2
C_OUT = 2 * KD
C_WQ = 2 * KD
FRONT = C_PROJ + C_PW + C_POOL + C_OUT + C_WQ
RAW = 4
PIECE = CHUNK // 2
SPLIT = 4
UP0 = FRONT + 2 * NKEYS
HALF = NKEYS // 2
TOK = 4
PLAIN_TILES = 32
ROUTE_TILE = 24
CONV_OPS = TAPS + 1
RANK_OPS = 32
RANK_READ = (6, 16)
TAIL_OPS = 19
STEPS = SEQ // TOK

V_MIX, V_PS, V_DW, V_DB, V_LG, V_LB, V_PB, V_FFN = 0, 16, 24, 272, 280, 288, 296, 304
V_COLS = 320


def bass_hymba_peer_block(nc, hT_d, x_d, front_d, down_d, up_d, keys_d, vec_d, fg_d, out_d):
    spill_d = nc.dram_tensor("residual", (P, TT, D), F32, kind="Internal").ap()
    base = nc.sbuf_base + (-nc.sbuf_base) % 64
    top = [base]

    def at(name, shape, dt, offset):
        return nc.alloc_sbuf_tensor_at(name, shape, dt, offset=offset)

    def place(name, shape, dt):
        n = 4
        for s in shape[1:]:
            n *= s
        offset = top[0]
        top[0] += n + (-n) % 32
        return at(name, shape, dt, offset), offset

    gated, o_gated = place("gated", [P, NKEYS, SEQ], F32)
    raw, o_raw = place("raw", [P, RAW, CHUNK], F32)
    wh, _ = place("wh", [P, SPLIT, PIECE], F32R)
    wl, _ = place("wl", [P, SPLIT, PIECE], F32R)
    xh, o_xh = place("xh", [P, KD, SEQ], F32R)
    xl, o_xl = place("xl", [P, KD, SEQ], F32R)
    ident, _ = place("ident", [P, P], F32)
    iota, _ = place("iota", [P, P], F32)
    one_j, o_one = place("one_j", [P, 2, TOK, P], F32)
    one_i, _ = place("one_i", [P, 2, TOK, HALF], F32)
    gelu, _ = place("gelu", [P, 2, SEQ], F32)
    slot_t, _ = place("slot_t", [P, 3, SEQ], F32)
    small, _ = place("small", [P, 16], F32)
    assert top[0] <= nc.sbuf_usable_end, (top[0], nc.sbuf_usable_end)
    ah = at("ah", [P, 2, SEQ], F32R, o_one)
    al = at("al", [P, 2, SEQ], F32R, o_one + 2048)

    def early(name, shape, offset, dt=F32):
        return at(name, shape, dt, o_gated + offset)

    hn = early("hn", [P, KD, T], 0)
    glu = early("glu", [P, CT, PAD + T], 17408)
    cv = early("cv", [P, CT, SEQ], 26624)
    xp = early("xp", [P, CT, T], 34816)
    sum_a = early("sum_a", [P, CT, T], 43520)
    sum_b = early("sum_b", [P, CT, T], 52224)
    sig = early("sig", [P, 2, T], 60928)
    odd = early("odd", [P, SEQ], 63232)
    pooled = early("pooled", [P, CT, SEQ], 65536)
    y = early("y", [P, KD, SEQ], 73728)
    cv_sq = early("cv_sq", [P, CT, SEQ], 73728)
    act_cv = early("act_cv", [P, CT, SEQ], 90112)
    res = early("res", [P, TT, D], 98304)
    sq = early("sq", [P, 2, T], 114688)
    rstd1 = early("rstd1", [P, T], 116864)
    rstd2 = early("rstd2", [P, SEQ], 118016)
    vec = early("vec", [P, V_COLS], 119040)
    ones = early("ones", [P, P], 120320)
    junk = early("junk", [P, D], 120832)
    xn = early("xn", [P, TT, D], 0)
    xT = early("xT", [P, KD, SEQ], 17408)
    keys = early("keys", [P, 2 * HEADS, NKEYS], 65536)
    qT = early("qT", [P, 2, SEQ], 73728)
    sv = early("sv", [P, TT, HEADS, 2, TOPK], 75776)
    si_u = early("si_u", [P, TT, HEADS, 2, TOPK], 77824, U32)
    si = early("si", [P, TT, HEADS, 2, TOPK], 79872)
    left = early("left", [P, TT, NKEYS], 81920)
    cand = early("cand", [P, TT, TOPK * TOPK], 82944)
    cand_left = early("cand_left", [P, TT, TOPK * TOPK], 84992)
    topv = early("topv", [P, TT, HEADS, TOPK], 87040)
    pos = early("pos", [P, TT, HEADS, TOPK], 88064, U32)
    pos_u = early("pos_u", [P, 2, TT * SLOTS], 89088, U32)
    pos_f = early("pos_f", [P, 2, TT * SLOTS], 91136)
    route = early("route", [P, 3, TT, SLOTS], 93184)
    norm = early("norm", [P, 2, TT * HEADS], 96256)
    match = early("match", [P, SLOTS, TOPK], 120832)
    res2 = at("res2", [P, TT, D], F32, o_xl)
    fg = at("fg", [P, D], F32, o_xh)
    junk2 = at("junk2", [P, D], F32, o_xh + 8192)
    outb = at("outb", [P, TT, D], F32, o_raw)

    ctx = ExitStack()
    ps = ctx.enter_context(nc.psum_tensor("ps", [P, 8, 512], F32))

    def sem(name):
        return ctx.enter_context(nc.semaphore(name))

    s_hT = [sem(f"hT_loaded{g}") for g in range(4)]
    s_raw = [sem(f"raw_loaded{s}") for s in range(RAW)]
    s_vec, s_x, s_keys, s_fg, s_res2 = sem("vec_loaded"), sem("x_loaded"), sem("keys_loaded"), sem("fg_loaded"), sem("res2_loaded")
    s_spill, s_out = sem("residual_spilled"), sem("out_stored")
    ones_ready, iota_ready, pad_ready, ident_ready = sem("ones_ready"), sem("iota_ready"), sem("pad_ready"), sem("ident_ready")
    front_used, wh_ready, wl_ready, piece_used = sem("front_used"), sem("wh_ready"), sem("wl_ready"), sem("piece_used")
    sq_ready, sq_used, var1, std1, rs1, hn_ready = sem("sq_ready"), sem("sq_used"), sem("var1"), sem("std1"), sem("rs1"), sem("hn_ready")
    sig_ready, glu_ready, tap_done = sem("sig_ready"), sem("glu_ready"), sem("tap_done")
    mean_done, xc_ready, cvsq_ready, var_done = sem("mean_done"), sem("xc_ready"), sem("cvsq_ready"), sem("var_done")
    var2, std2, rs2, ln_ready, silu_ready = sem("var2"), sem("std2"), sem("rs2"), sem("ln_ready"), sem("silu_ready")
    xp_ready, pool_step, pooled_ready = sem("xp_ready"), sem("pool_step"), sem("pooled_ready")
    y_ready, res_ready = sem("y_ready"), sem("res_ready")
    ssq3, var3, std3, rs3, xn_ready = sem("ssq3"), sem("var3"), sem("std3"), sem("rs3"), sem("xn_ready")
    xT_ps, xT_ready, xh_ready, xl_ready = sem("xT_ps"), sem("xT_ready"), sem("xh_ready"), sem("xl_ready")
    q_ready, score_done, rank = sem("q_ready"), sem("score_done"), sem("rank")
    z_ready, e_ready, tail, route_ps, slot_ready = sem("z_ready"), sem("e_ready"), sem("tail"), sem("route_ps"), sem("slot_ready")
    gelu_ready, tile_ready = sem("gelu_ready"), sem("tile_ready")
    eq_ready, onehot_ready, g_done, g_read = sem("eq_ready"), sem("onehot_ready"), sem("g_done"), sem("g_read")
    ah_ready, al_ready = sem("ah_ready"), sem("al_ready")
    h3_ready, ssq4, var4, std4, rs4, fin = sem("h3_ready"), sem("ssq4"), sem("var4"), sem("std4"), sem("rs4"), sem("fin")
    block = ctx.enter_context(nc.Block())

    def chunk(table, index):
        return table[bass.ds(index, 1)].rearrange("a p f -> (a p) f")

    def loads(c):
        return 16 * (c // RAW + 1)

    def gated_tile(i):
        return gated[:, bass.ds(i, 1), :].rearrange("p a t -> p (a t)")

    def bcast(ap, count):
        return ap.rearrange("p (n o) -> p n o", o=1).broadcast_to((P, ap.shape[1], count))

    @block.sync
    def _(sp):
        for g in range(4):
            sp.dma_start(hn[:, 4 * g:4 * g + 4, :], hT_d[:, 4 * g:4 * g + 4, :]).then_inc(s_hT[g], 16)
            if g == 0:
                sp.dma_start(vec[:], vec_d).then_inc(s_vec, 16)
        for c in range(RAW):
            sp.dma_start(raw[:, c, :], chunk(front_d, c)).then_inc(s_raw[c], 16)
        sp.dma_start(res[:], x_d).then_inc(s_x, 16)
        groups = (C_PROJ + C_PW + C_POOL) // RAW
        with sp.Fori(1, groups) as it:
            for u in range(RAW):
                sp.wait_ge(front_used, it * RAW + (u + 1 - RAW))
                sp.dma_start(raw[:, u, :], chunk(front_d, it * RAW + u)).then_inc(s_raw[u], 16)
        for c in range(RAW * groups, RAW * groups + RAW):
            sp.wait_ge(front_used, c - RAW + 1)
            sp.dma_start(raw[:, c % RAW, :], chunk(front_d, c)).then_inc(s_raw[c % RAW], 16)
        sp.wait_ge(front_used, C_PROJ + C_PW + C_POOL)
        sp.dma_start(keys[:], keys_d).then_inc(s_keys, 16)
        with sp.Fori(groups + 1, FRONT // RAW) as it:
            for u in range(RAW):
                sp.wait_ge(front_used, it * RAW + (u + 1 - RAW))
                sp.dma_start(raw[:, u, :], chunk(front_d, it * RAW + u)).then_inc(s_raw[u], 16)
        for c in range(FRONT - FRONT % RAW, FRONT + RAW):
            table, first = (front_d, 0) if c < FRONT else (down_d, FRONT)
            sp.wait_ge(front_used, c - RAW + 1)
            sp.dma_start(raw[:, c % RAW, :], chunk(table, c - first)).then_inc(s_raw[c % RAW], 16)
        for table, first, skip in ((down_d, FRONT, 1), (up_d, UP0, 0)):
            with sp.Fori(skip, 2 * NKEYS // RAW) as it:
                for u in range(RAW):
                    slot = (first + u) % RAW
                    sp.wait_ge(wl_ready, it * (2 * RAW) + 2 * (first - FRONT + u - RAW) + 2)
                    sp.dma_start(raw[:, slot, :], chunk(table, it * RAW + u)).then_inc(s_raw[slot], 16)
        for t in range(TT):
            sp.wait_ge(fin, t + 1)
            sp.dma_start(out_d[t], outb[:, t, :]).then_inc(s_out, 16)
        sp.wait_ge(s_out, 16 * TT)

    @block.gpsimd
    def _(pool):
        nc.gpsimd.memset(ones[:], 1.0).then_inc(ones_ready, 1)
        nc.gpsimd.memset(glu[:, :, 0:PAD], 0.0).then_inc(pad_ready, 1)
        nc.gpsimd.iota(iota[:], [[1, P]], base=0, channel_multiplier=0,
                       allow_small_or_imprecise_dtypes=True).then_inc(iota_ready, 1)
        nc.gpsimd.iota(small[:, 0:1], [[0, 1]], base=0, channel_multiplier=1,
                       allow_small_or_imprecise_dtypes=True).then_inc(iota_ready, 1)
        step = 0
        for g, window in enumerate(WINDOWS):
            tiles = slice(2 * g, 2 * g + 2)
            pool.wait_ge(xp_ready, 2 * g + 2)
            src, span = xp, 1
            while span < window:
                dst = sum_b if src is sum_a else sum_a
                lo = 2 * span - 1
                nc.gpsimd.tensor_tensor(dst[:, tiles, lo:T], src[:, tiles, lo:T], src[:, tiles, lo - span:T - span],
                                        ALU.add).then_inc(pool_step, 1)
                step += 1
                pool.wait_ge(pool_step, step)
                src, span = dst, 2 * span
            dst = sum_b if src is sum_a else sum_a
            nc.gpsimd.tensor_scalar(dst[:, tiles, META:T], src[:, tiles, META:T], 1.0 / window, None,
                                    ALU.mult).then_inc(pool_step, 1)
            step += 1
            pool.wait_ge(pool_step, step)
            nc.gpsimd.tensor_tensor(pooled[:, tiles, :], dst[:, tiles, META:T], xp[:, tiles, META:T],
                                    ALU.subtract).then_inc(pooled_ready, 1)
        for k in range(KD):
            pool.wait_ge(xh_ready, k + 1)
            nc.gpsimd.tensor_tensor(xl[:, k, :], xT[:, k, :], xh[:, k, :].bitcast(F32), ALU.subtract).then_inc(xl_ready, 1)

    @block.scalar
    def _(act):
        for k in range(KD):
            if k % 4 == 0:
                act.wait_ge(s_hT[k // 4], 16)
            if k >= 2:
                act.wait_ge(sq_used, k - 1)
            nc.scalar.activation(sq[:, k % 2, :], hn[:, k, :], ACT.Square).then_inc(sq_ready, 1)
        act.wait_ge(var1, 1)
        nc.scalar.activation(rstd1[:], rstd1[:], ACT.Sqrt).then_inc(std1, 1)

        def glu_gate(c, u):
            act.wait_ge(front_used, c * 4 + 4)
            nc.scalar.activation(sig[:, u, :], ps[:, 2 * u + 1, 0:T], ACT.Sigmoid).then_inc(sig_ready, 1)

        for u in range(2):
            glu_gate(u, u)
        with act.Fori(1, CT // 2) as it:
            for u in range(2):
                act.wait_ge(glu_ready, it * 2 + (u - 1))
                glu_gate(it * 2 + u, u)

        def keep_xp(n):
            act.wait_ge(front_used, 2 * (2 * CT + n + 1))
            nc.scalar.activation(xp[:, n, :], ps[:, n % 4, 0:T], ACT.Copy).then_inc(xp_ready, 1)

        for n in range(4):
            keep_xp(n)
        act.wait_ge(xc_ready, 1)
        nc.scalar.activation(cv_sq[:], cv[:], ACT.Square).then_inc(cvsq_ready, 1)
        for n in range(4, 6):
            keep_xp(n)
        act.wait_ge(var2, 1)
        nc.scalar.activation(rstd2[:], rstd2[:], ACT.Sqrt).then_inc(std2, 1)
        act.wait_ge(ln_ready, 1)
        for k in range(CT):
            nc.scalar.activation(act_cv[:, k, :], cv[:, k, :], ACT.Silu, bias=vec[:, V_LB + k:V_LB + k + 1],
                                 scale=vec[:, V_LG + k:V_LG + k + 1]).then_inc(silu_ready, 1)
        for n in range(6, 8):
            keep_xp(n)
        for m in range(CT):
            act.wait_ge(front_used, C_PROJ + m + 1)
            nc.scalar.activation(y[:, CT + m, :], ps[:, m % 4, 0:SEQ], ACT.Identity,
                                 bias=vec[:, V_PB + m:V_PB + m + 1]).then_inc(y_ready, 1)
        for m in range(CT):
            act.wait_ge(front_used, C_PROJ + C_PW + m // 4 + 1)
            nc.scalar.activation(y[:, m, :], ps[:, m % 4, 0:SEQ], ACT.Copy,
                                 scale=vec[:, V_PS + m:V_PS + m + 1]).then_inc(y_ready, 1)
        for t in range(TT):
            act.wait_ge(res_ready, 4 + 2 * t + 2)
            if t:
                act.wait_ge(ssq3, t)
            nc.scalar.activation(junk[:], res[:, t, :], ACT.Square, accum_out=small[:, 2 + t:3 + t]).then_inc(ssq3, 1)
        act.wait_ge(var3, 1)
        nc.scalar.activation(small[:, 2:4], small[:, 2:4], ACT.Sqrt).then_inc(std3, 1)
        act.dma_start(spill_d, res[:]).then_inc(s_spill, 16)
        for k in range(KD):
            act.wait_ge(xT_ps, k - k % 2 + 2)
            nc.scalar.activation(xT[:, k, :], ps[:, k // 2, (k % 2) * SEQ:(k % 2) * SEQ + SEQ], ACT.Copy,
                                 scale=vec[:, V_FFN + k:V_FFN + k + 1]).then_inc(xT_ready, 1)
        act.wait_ge(xT_ready, KD)
        for k in range(KD):
            nc.scalar.activation(xh[:, k, :], xT[:, k, :], ACT.Copy).then_inc(xh_ready, 1)

        def query(n, u):
            act.wait_ge(front_used, n * 2 + (FRONT - C_WQ + 2))
            nc.scalar.activation(qT[:, u, :], ps[:, u, 0:SEQ], ACT.Copy).then_inc(q_ready, 1)

        for u in range(2):
            query(u, u)
        with act.Fori(1, HEADS) as it:
            for u in range(2):
                act.wait_ge(score_done, it * 2 + (u - 1))
                query(it * 2 + u, u)

        def high(first, it, u, reused=True):
            for part in range(4):
                c = first + 2 * u + part // 2
                act.wait_ge(s_raw[c % RAW], it * 16 + loads(c))
                if reused:
                    act.wait_ge(piece_used, it * 8 + (2 * (c - FRONT) + part % 2 - SPLIT + 1))
                nc.scalar.activation(wh[:, part, :], raw[:, c % RAW, (part % 2) * PIECE:(part % 2 + 1) * PIECE],
                                     ACT.Copy).then_inc(wh_ready, 1)

        def gelu_into(out, i, u):
            act.wait_ge(piece_used, i * 4 + 4)
            nc.scalar.activation(out, ps[:, u, 0:SEQ], ACT.Gelu).then_inc(gelu_ready, 1)

        high(FRONT, 0, 0, reused=False)
        act.wait_ge(z_ready, 1)
        nc.scalar.activation(route[:, 2], route[:, 2], ACT.Exp).then_inc(e_ready, 1)
        high(FRONT, 0, 1)
        act.wait_ge(s_spill, 16)
        gelu_into(gated_tile(0), 0, 0)

        def direct_tiles(lo, hi):
            with act.Fori(lo // 2, hi // 2) as it:
                for u in range(2):
                    high(FRONT, it, u)
                    gelu_into(gated_tile(it * 2 + (u - 1)), it * 2 + (u - 1), (u + 1) % 2)

        direct_tiles(2, ROUTE_TILE)
        act.wait_ge(route_ps, 1)
        for r in range(3):
            nc.scalar.activation(slot_t[:, r, :], ps[:, 4 + r, 0:SEQ], ACT.Copy).then_inc(slot_ready, 1)
        direct_tiles(ROUTE_TILE, HALF)
        high(FRONT, HALF // 2, 0)
        gelu_into(gated_tile(HALF - 1), HALF - 1, 1)
        for i in (HALF + 1, HALF + 2, HALF + 3):
            high(FRONT, i // 2, i % 2)
            if i > HALF + 2:
                act.wait_ge(tile_ready, i - HALF - 2)
            gelu_into(gelu[:, (i - 1) % 2, :], i - 1, (i - 1) % 2)
        with act.Fori(HALF // 2 + 2, NKEYS // 2) as it:
            for u in range(2):
                high(FRONT, it, u)
                act.wait_ge(tile_ready, it * 2 + (u - HALF - 2))
                gelu_into(gelu[:, (u + 1) % 2, :], it * 2 + (u - 1), (u + 1) % 2)

        def high_gated(i, u):
            nc.scalar.activation(ah[:, u, :], gated_tile(i), ACT.Copy).then_inc(ah_ready, 1)

        high(UP0, 0, 0)
        act.wait_ge(tile_ready, HALF - 2)
        gelu_into(gelu[:, 1, :], NKEYS - 1, 1)
        act.dma_start(res2[:], spill_d).then_inc(s_res2, 16)
        act.dma_start(fg[:], fg_d).then_inc(s_fg, 16)
        act.wait_ge(g_read, 2 * STEPS)
        for i in range(2):
            high_gated(i, i)
        high(UP0, 0, 1)
        act.wait_ge(tile_ready, NKEYS - HALF)
        high_gated(2, 0)
        with act.Fori(1, NKEYS // 2 - 1) as it:
            for u in range(2):
                high(UP0, it, u)
                high_gated(it * 2 + (u + 1), (u + 1) % 2)
        high(UP0, NKEYS // 2 - 1, 0)
        high_gated(NKEYS - 1, 1)
        high(UP0, NKEYS // 2 - 1, 1)
        for t in range(TT):
            act.wait_ge(h3_ready, 4 * t + 4)
            if t:
                act.wait_ge(ssq4, t)
            nc.scalar.activation(junk2[:], res2[:, t, :], ACT.Square, accum_out=small[:, 6 + t:7 + t]).then_inc(ssq4, 1)
            act.wait_ge(var4, t + 1)
            nc.scalar.activation(small[:, 6 + t:7 + t], small[:, 6 + t:7 + t], ACT.Sqrt).then_inc(std4, 1)

    @block.tensor
    def _(pe):
        matmul = nc.tensor.matmul
        pe.wait_ge(ones_ready, 1)
        for k in range(KD):
            pe.wait_ge(sq_ready, k + 1)
            matmul(ps[:, 4, 0:T], ones[:], sq[:, k % 2, :], start=(k == 0), stop=(k == KD - 1)).then_inc(sq_used, 1)

        def proj_tile(it, u, first=False):
            for half in range(2):
                c = 2 * u + half
                pe.wait_ge(s_raw[c % RAW], it * 32 + loads(c))
                for k in range(8):
                    kk = 8 * half + k
                    if first:
                        pe.wait_ge(hn_ready, kk + 1)
                    m = matmul(ps[:, u, 0:T], raw[:, c % RAW, k * P:(k + 1) * P], hn[:, kk, :],
                               start=(kk == 0), stop=(kk == KD - 1))
                m.then_inc(front_used, 1)

        for u in range(4):
            proj_tile(0, u, first=(u == 0))
        with pe.Fori(1, 2 * CT // 4) as it:
            for u in range(4):
                if u % 2 == 0:
                    pe.wait_ge(glu_ready, it * 2 + (u // 2 - 1))
                proj_tile(it, u)
        for u in range(4):
            if u % 2 == 0:
                pe.wait_ge(glu_ready, CT + u // 2 - 1)
            proj_tile(4, u)
        for k in range(CT):
            pe.wait_ge(tap_done, CONV_OPS * (k + 1))
            m = matmul(ps[:, 5, 0:SEQ], ones[:], cv[:, k, :], start=(k == 0), stop=(k == CT - 1))
        m.then_inc(mean_done, 1)
        for u in range(2):
            pe.wait_ge(xp_ready, u + 1)
            proj_tile(5, u)
        pe.wait_ge(cvsq_ready, 1)
        for k in range(CT):
            m = matmul(ps[:, 6, 0:SEQ], ones[:], cv_sq[:, k, :], start=(k == 0), stop=(k == CT - 1))
        m.then_inc(var_done, 1)
        for u in range(2, 4):
            pe.wait_ge(xp_ready, u + 1)
            proj_tile(5, u)

        for m in range(CT):
            c = C_PROJ + m
            pe.wait_ge(s_raw[c % RAW], loads(c))
            if m < 4:
                pe.wait_ge(xp_ready, 5 + m)
            else:
                pe.wait_ge(y_ready, m - 3)
            for k in range(CT):
                pe.wait_ge(silu_ready, k + 1)
                last = matmul(ps[:, m % 4, 0:SEQ], raw[:, c % RAW, k * P:(k + 1) * P], act_cv[:, k, :],
                              start=(k == 0), stop=(k == CT - 1))
            last.then_inc(front_used, 1)
        for q in range(C_POOL):
            c = C_PROJ + C_PW + q
            pe.wait_ge(s_raw[c % RAW], loads(c))
            for g in (2 * q, 2 * q + 1):
                pe.wait_ge(pooled_ready, g + 1)
                for d in range(2):
                    m = 2 * g + d
                    pe.wait_ge(y_ready, CT + m - 3)
                    for k in range(2):
                        block_at = ((g % 2 * 2 + d) * 2 + k) * P
                        last = matmul(ps[:, m % 4, 0:SEQ], raw[:, c % RAW, block_at:block_at + P],
                                      pooled[:, 2 * g + k, :], start=(k == 0), stop=(k == 1))
            last.then_inc(front_used, 1)

        for half in range(2):
            for n in range(KD):
                k = (n + CT) % KD
                c = C_PROJ + C_PW + C_POOL + half * KD + n
                pe.wait_ge(s_raw[c % RAW], loads(c))
                pe.wait_ge(y_ready, n + 1 if half == 0 else KD)
                for t in range(TT):
                    for w in range(2):
                        last = matmul(ps[:, 4 * (1 - half) + 2 * t + w, :], y[:, k, t * P:(t + 1) * P],
                                      raw[:, c % RAW, w * 512:(w + 1) * 512], start=(n == 0), stop=(n == KD - 1))
                last.then_inc(front_used, 1)

        pe.wait_ge(ident_ready, 1)
        for k in range(KD):
            for t in range(TT):
                pe.wait_ge(xn_ready, TT if k else t + 1)
                at_ = (k % 2) * SEQ + t * P
                last = nc.tensor.transpose(ps[:, k // 2, at_:at_ + P], xn[:, t, k * P:(k + 1) * P], ident[:])
            last.then_inc(xT_ps, 1)

        def query(it, v, first=False):
            for half in range(2):
                c = FRONT - C_WQ + 2 * v + half
                pe.wait_ge(s_raw[c % RAW], it * 32 + loads(c))
                if half == 0 and not (first and v < 2):
                    pe.wait_ge(q_ready, it * 4 + (v - 1))
                for k in range(8):
                    kk = 8 * half + k
                    if first and v == 0:
                        pe.wait_ge(xT_ready, max(kk + 1, 4))
                    m = matmul(ps[:, v % 2, 0:SEQ], raw[:, c % RAW, k * P:(k + 1) * P], xT[:, kk, :],
                               start=(kk == 0), stop=(kk == KD - 1))
                m.then_inc(front_used, 1)

        def scores(it, v, first=False):
            head, half = v // 2, v % 2
            pe.wait_ge(q_ready, it * 4 + (v + 1))
            if not first:
                pe.wait_ge(rank, it * (2 * RANK_OPS) + ((head - 2) * RANK_OPS + RANK_READ[half]))
            for t in range(TT):
                key = keys[:, bass.ds(it * 4 + v, 1), :].rearrange("p a n -> p (a n)")
                m = matmul(ps[:, 2 + v, t * P:(t + 1) * P], qT[:, half, t * P:(t + 1) * P], key, start=True, stop=True)
            m.then_inc(score_done, 1)

        query(0, 0, first=True)
        pe.wait_ge(s_keys, 16)
        for v in range(1, 4):
            query(0, v, first=True)
            scores(0, v - 1, first=True)

        def queries(it, first=False):
            query(it, 0)
            scores(it - 1, 3, first=first)
            for v in range(1, 4):
                query(it, v)
                scores(it, v - 1)

        queries(1, first=True)
        with pe.Fori(2, HEADS // 2) as it:
            queries(it)
        scores(HEADS // 2 - 1, 3)

        def down_tile(it, u, first=False):
            if not first:
                pe.wait_ge(gelu_ready, it * 2 + (u - 1))
            for part in range(4):
                pe.wait_ge(wl_ready, it * 8 + (4 * u + part + 1))
                for k in range(4):
                    kk = 4 * part + k
                    if first and u == 0:
                        pe.wait_ge(xl_ready, kk + 1)
                    cols = slice(k * P, (k + 1) * P)
                    matmul(ps[:, u, 0:SEQ], wh[:, part, cols], xh[:, kk, :], start=(kk == 0), stop=False)
                    matmul(ps[:, u, 0:SEQ], wh[:, part, cols], xl[:, kk, :], start=False, stop=False)
                    m = matmul(ps[:, u, 0:SEQ], wl[:, part, cols], xh[:, kk, :], start=False, stop=(kk == KD - 1))
                m.then_inc(piece_used, 1)

        def gate_step(s, u, first=False):
            if not first:
                pe.wait_ge(g_read, s - 1)
            pe.wait_ge(onehot_ready, s + 1)
            for n in range(TOK):
                m = matmul(ps[:, 2 + u, n * HALF:(n + 1) * HALF], one_j[:, u, n, :], one_i[:, u, n, :], start=True, stop=True)
            m.then_inc(g_done, 1)

        for u in range(2):
            down_tile(0, u, first=True)
        with pe.Fori(1, ROUTE_TILE // 2) as it:
            for u in range(2):
                down_tile(it, u)
        pe.wait_ge(tail, TAIL_OPS)
        for r in range(3):
            for t in range(TT):
                m = nc.tensor.transpose(ps[:, 4 + r, t * P:(t + 1) * P], route[:, r, t, :], ident[:])
        m.then_inc(route_ps, 1)
        with pe.Fori(ROUTE_TILE // 2, PLAIN_TILES // 2) as it:
            for u in range(2):
                down_tile(it, u)
        down_tile(PLAIN_TILES // 2, 0)
        for u in range(2):
            gate_step(u, u, first=True)
        down_tile(PLAIN_TILES // 2, 1)
        for u in range(2):
            gate_step(2 + u, u)
        with pe.Fori(PLAIN_TILES // 2 + 1, HALF // 2) as it:
            for u in range(2):
                down_tile(it, u)
                for v in range(2):
                    gate_step(it * 4 + (2 * u + v - 2 * PLAIN_TILES), v)
        with pe.Fori(HALF // 2, NKEYS // 2) as it:
            for u in range(2):
                down_tile(it, u)
                gate_step(it * 2 + u, u)

        def up_tile(it, u, start=False, stop=False):
            pe.wait_ge(al_ready, it * 2 + (u + 1))
            for part in range(4):
                pe.wait_ge(wl_ready, it * 8 + (4 * NKEYS + 4 * u + part + 1))
                for t in range(TT):
                    tok = slice(t * P, (t + 1) * P)
                    matmul(ps[:, 4 * t + part, :], ah[:, u, tok], wh[:, part, :], start=start, stop=False)
                    matmul(ps[:, 4 * t + part, :], ah[:, u, tok], wl[:, part, :], start=False, stop=False)
                    m = matmul(ps[:, 4 * t + part, :], al[:, u, tok], wh[:, part, :], start=False, stop=stop)
                m.then_inc(piece_used, 1)

        pe.wait_ge(gelu_ready, NKEYS)
        pe.wait_ge(g_read, 2 * STEPS)
        up_tile(0, 0, start=True)
        up_tile(0, 1)
        with pe.Fori(1, NKEYS // 2 - 1) as it:
            for u in range(2):
                up_tile(it, u)
        up_tile(NKEYS // 2 - 1, 0)
        up_tile(NKEYS // 2 - 1, 1, stop=True)

    @block.vector
    def _(dve):
        v_ = nc.vector
        dve.wait_ge(iota_ready, 2)
        v_.tensor_scalar(ident[:], iota[:], small[:, 0:1], None, ALU.is_equal).then_inc(ident_ready, 1)
        dve.wait_ge(sq_used, KD)
        v_.tensor_scalar(rstd1[:], ps[:, 4, 0:T], 1.0 / D, RMS_EPS, ALU.mult, ALU.add).then_inc(var1, 1)
        dve.wait_ge(std1, 1)
        v_.reciprocal(rstd1[:], rstd1[:]).then_inc(rs1, 1)
        dve.wait_ge(s_vec, 16)
        dve.wait_ge(rs1, 1)
        for k in range(KD):
            v_.scalar_tensor_tensor(out=hn[:, k, :], in0=hn[:, k, :], scalar=vec[:, V_MIX + k:V_MIX + k + 1], in1=rstd1[:],
                                    op0=ALU.mult, op1=ALU.mult).then_inc(hn_ready, 1)

        def conv_tile(c, u):
            dve.wait_ge(sig_ready, c + 1)
            v_.tensor_tensor(glu[:, bass.ds(c, 1), PAD:PAD + T].rearrange("p a t -> p (a t)"), ps[:, 2 * u, 0:T],
                             sig[:, u, :], ALU.mult).then_inc(glu_ready, 1)
            dve.wait_ge(glu_ready, c + 1)
            acc = cv[:, bass.ds(c, 1), :].rearrange("p a t -> p (a t)")
            for j in range(TAPS):
                x = glu[:, bass.ds(c, 1), j:j + SEQ].rearrange("p a t -> p (a t)")
                w = vec[:, bass.ds(c * TAPS + (V_DW + j), 1)]
                if j >= 2:
                    dve.wait_ge(tap_done, c * CONV_OPS + (j - 1))
                if j == 0:
                    ins = v_.tensor_scalar(acc, x, w, vec[:, bass.ds(c + V_DB, 1)], ALU.mult, ALU.add)
                elif j == 1:
                    ins = v_.tensor_scalar(odd[:], x, w, None, ALU.mult)
                else:
                    dst = odd[:] if j % 2 else acc
                    ins = v_.scalar_tensor_tensor(out=dst, in0=x, scalar=w, in1=dst, op0=ALU.mult, op1=ALU.add)
                ins.then_inc(tap_done, 1)
            dve.wait_ge(tap_done, c * CONV_OPS + TAPS)
            v_.tensor_tensor(acc, acc, odd[:], ALU.add).then_inc(tap_done, 1)
            dve.wait_ge(tap_done, c * CONV_OPS + CONV_OPS)

        dve.wait_ge(pad_ready, 1)
        with dve.Fori(0, CT // 2) as it:
            for u in range(2):
                conv_tile(it * 2 + u, u)
        dve.wait_ge(mean_done, 1)
        mean = ps[:, 5:6, 0:SEQ].broadcast_to((P, CT, SEQ))
        v_.scalar_tensor_tensor(out=cv[:], in0=mean, scalar=-1.0 / W, in1=cv[:], op0=ALU.mult, op1=ALU.add).then_inc(xc_ready, 1)
        dve.wait_ge(var_done, 1)
        v_.tensor_scalar(rstd2[:], ps[:, 6, 0:SEQ], 1.0 / W, LN_EPS, ALU.mult, ALU.add).then_inc(var2, 1)
        dve.wait_ge(std2, 1)
        v_.reciprocal(rstd2[:], rstd2[:]).then_inc(rs2, 1)
        dve.wait_ge(rs2, 1)
        v_.tensor_tensor(cv[:], cv[:], rstd2[:].rearrange("p (a t) -> p a t", a=1).broadcast_to((P, CT, SEQ)),
                         ALU.mult).then_inc(ln_ready, 1)
        dve.wait_ge(s_x, 16)
        for half in range(2):
            dve.wait_ge(front_used, C_PROJ + C_PW + C_POOL + (half + 1) * KD)
            for t in range(TT):
                for w in range(2):
                    part = res[:, t, half * 1024 + w * 512:half * 1024 + w * 512 + 512]
                    v_.tensor_tensor(part, part, ps[:, 4 * (1 - half) + 2 * t + w, :], ALU.add).then_inc(res_ready, 1)
        dve.wait_ge(ssq3, TT)
        v_.tensor_scalar(small[:, 2:4], small[:, 2:4], 1.0 / D, RMS_EPS, ALU.mult, ALU.add).then_inc(var3, 1)
        dve.wait_ge(std3, 1)
        v_.reciprocal(small[:, 2:4], small[:, 2:4]).then_inc(rs3, 1)
        dve.wait_ge(rs3, 1)
        for t in range(TT):
            v_.tensor_scalar(xn[:, t, :], res[:, t, :], small[:, 2 + t:3 + t], None, ALU.mult).then_inc(xn_ready, 1)

        done = [0]

        def ranked(ins):
            ins.then_inc(rank, 1)
            done[0] += 1
            if done[0] >= 2:
                dve.wait_ge(rank, done[0] - 1)

        def top16(values, indices, source, rest):
            for t in range(TT):
                ranked(v_.max(values(t)[:, 0:8], source(t)))
            for t in range(TT):
                ranked(v_.max_index(indices(t)[:, 0:8], values(t)[:, 0:8], source(t)))
            for t in range(TT):
                ranked(v_.match_replace(rest(t), values(t)[:, 0:8], source(t), LOWEST))
            for t in range(TT):
                ranked(v_.max(values(t)[:, 8:16], rest(t)))
            for t in range(TT):
                ranked(v_.max_index(indices(t)[:, 8:16], values(t)[:, 8:16], rest(t)))

        for h in range(HEADS):
            for half in range(2):
                dve.wait_ge(score_done, 2 * h + half + 1)
                top16(lambda t: sv[:, t, h, half, :], lambda t: si_u[:, t, h, half, :],
                      lambda t: ps[:, 2 + h % 2 * 2 + half, t * P:(t + 1) * P], lambda t: left[:, t, :])
            for t in range(TT):
                first = bcast(sv[:, t, h, 0, :], TOPK)
                second = sv[:, t, h, 1:2, :].broadcast_to((P, TOPK, TOPK))
                ranked(v_.tensor_tensor(cand[:, t, :].rearrange("p (a b) -> p a b", a=TOPK), first, second, ALU.add))
            top16(lambda t: topv[:, t, h, :], lambda t: pos[:, t, h, :], lambda t: cand[:, t, :], lambda t: cand_left[:, t, :])
            assert done[0] == RANK_OPS * (h + 1)
        dve.wait_ge(rank, RANK_OPS * HEADS)

        def low(it, u, parts=range(4)):
            for part in parts:
                slot = (FRONT + 2 * u + part // 2) % RAW
                dve.wait_ge(wh_ready, it * 8 + (4 * u + part + 1))
                v_.tensor_tensor(wl[:, part, :], raw[:, slot, (part % 2) * PIECE:(part % 2 + 1) * PIECE],
                                 wh[:, part, :].bitcast(F32), ALU.subtract).then_inc(wl_ready, 1)

        steps = [0]

        def tailed(ins):
            ins.then_inc(tail, 1)
            steps[0] += 1

        flat = "p t h k -> p (t h k)"
        top = topv[:].rearrange("p t h k -> p (t h) k")
        exp_ = route[:, 2].rearrange("p t (h k) -> p (t h) k", h=HEADS)
        v_.tensor_tensor(exp_, top, top[:, :, 0:1].broadcast_to((P, TT * HEADS, TOPK)), ALU.subtract).then_inc(z_ready, 1)
        low(0, 0)
        tailed(v_.tensor_copy(si[:].rearrange("p t h c k -> p (t h c k)"), si_u[:].rearrange("p t h c k -> p (t h c k)")))
        tailed(v_.tensor_scalar(pos_u[:, 0, :], pos[:].rearrange(flat), 4, None, ALU.logical_shift_right))
        tailed(v_.tensor_scalar(pos_u[:, 1, :], pos[:].rearrange(flat), TOPK - 1, None, ALU.bitwise_and))
        low(0, 1)
        dve.wait_ge(tail, 3)
        tailed(v_.tensor_copy(pos_f[:], pos_u[:]))
        dve.wait_ge(e_ready, 1)
        tailed(v_.tensor_reduce(norm[:, 0, :], exp_, AX.X, ALU.add))
        low(1, 0)
        dve.wait_ge(tail, 5)
        tailed(v_.reciprocal(norm[:, 1, :], norm[:, 0, :]))
        low(1, 1)
        dve.wait_ge(tail, 6)
        tailed(v_.tensor_tensor(exp_, exp_, bcast(norm[:, 1, :], TOPK), ALU.mult))
        tile = 4
        for r in range(2):
            for t in range(TT):
                low(tile // 2, 0)
                dve.wait_ge(tail, steps[0])
                tailed(v_.tensor_tensor(match[:], bcast(pos_f[:, r, t * SLOTS:(t + 1) * SLOTS], TOPK),
                                        iota[:, 0:TOPK].rearrange("p (a n) -> p a n", a=1).broadcast_to((P, SLOTS, TOPK)),
                                        ALU.is_equal))
                low(tile // 2, 1)
                dve.wait_ge(tail, steps[0])
                by_head = match[:].rearrange("p (h k) n -> p h k n", h=HEADS)
                index = si[:, t, :, r:r + 1, :].broadcast_to((P, HEADS, TOPK, TOPK))
                tailed(v_.tensor_tensor(by_head, by_head, index, ALU.mult))
                low(tile // 2 + 1, 0)
                dve.wait_ge(tail, steps[0])
                tailed(v_.tensor_reduce(route[:, r, t, :], match[:], AX.X, ALU.add))
                low(tile // 2 + 1, 1)
                tile += 4
        assert steps[0] == TAIL_OPS and tile == 20

        def plain(lo, hi):
            with dve.Fori(lo // 2, hi // 2) as it:
                for u in range(2):
                    low(it, u)

        def onehots(s, u, half, first=False):
            if not first:
                dve.wait_ge(g_done, s - 1)
            tok = bass.ds((s - (STEPS if half == 0 else 0)) * TOK, TOK)
            iota_i = iota[:, half * HALF:(half + 1) * HALF].rearrange("p (a n) -> p a n", a=1).broadcast_to((P, TOK, HALF))
            iota_j = iota[:].rearrange("p (a n) -> p a n", a=1).broadcast_to((P, TOK, P))
            v_.tensor_tensor(one_i[:, u], iota_i, bcast(slot_t[:, 0, tok], HALF), ALU.is_equal).then_inc(eq_ready, 1)
            v_.tensor_tensor(one_j[:, u], iota_j, bcast(slot_t[:, 1, tok], P), ALU.is_equal).then_inc(eq_ready, 1)
            dve.wait_ge(eq_ready, s * 2 + 2)
            v_.tensor_tensor(one_i[:, u], one_i[:, u], bcast(slot_t[:, 2, tok], HALF), ALU.mult).then_inc(onehot_ready, 1)

        def take(s, u, half):
            dve.wait_ge(g_done, s + 1)
            dst = gated[:, half * HALF:(half + 1) * HALF, bass.ds((s - (STEPS if half == 0 else 0)) * TOK, TOK)]
            got = ps[:, 2 + u, 0:TOK * HALF].rearrange("p (t i) -> p i t", t=TOK)
            if half:
                v_.tensor_copy(dst, got).then_inc(g_read, 1)
            else:
                v_.tensor_tensor(dst, dst, got, ALU.mult).then_inc(g_read, 1)

        def meet(i, u):
            dve.wait_ge(gelu_ready, i + 1)
            v_.tensor_tensor(gated_tile(i), gated_tile(i), gelu[:, u, :], ALU.mult).then_inc(tile_ready, 1)

        plain(20, PLAIN_TILES)
        dve.wait_ge(slot_ready, 3)
        for i in (PLAIN_TILES, PLAIN_TILES + 1):
            for v in range(2):
                s = 2 * (i - PLAIN_TILES) + v
                low(i // 2, i % 2, (2 * v,))
                onehots(s, v, 1, first=(s < 2))
                low(i // 2, i % 2, (2 * v + 1,))
                if s:
                    take(s - 1, 1 - v, 1)
        with dve.Fori(PLAIN_TILES // 2 + 1, HALF // 2) as it:
            for u in range(2):
                for v in range(2):
                    s = it * 4 + (2 * u + v - 2 * PLAIN_TILES)
                    low(it, u, (2 * v,))
                    onehots(s, v, 1)
                    low(it, u, (2 * v + 1,))
                    take(s - 1, 1 - v, 1)
        low(HALF // 2, 0, (0, 1))
        onehots(STEPS, 0, 0)
        low(HALF // 2, 0, (2, 3))
        take(STEPS - 1, 1, 1)
        dve.wait_ge(gelu_ready, HALF)
        dve.wait_ge(g_read, STEPS)
        low(HALF // 2, 1, (0, 1))
        onehots(STEPS + 1, 1, 0)
        low(HALF // 2, 1, (2, 3))
        take(STEPS, 0, 0)
        meet(HALF, 0)
        with dve.Fori(HALF // 2 + 1, NKEYS // 2) as it:
            for u in range(2):
                low(it, u, (0, 1))
                onehots(it * 2 + u, u, 0)
                low(it, u, (2, 3))
                take(it * 2 + (u - 1), 1 - u, 0)
                meet(it * 2 + (u - 1), 1 - u)

        def low_gated(i, u):
            dve.wait_ge(ah_ready, i + 1)
            v_.tensor_tensor(al[:, u, :], gated_tile(i), ah[:, u, :].bitcast(F32), ALU.subtract).then_inc(al_ready, 1)

        half_up = NKEYS // 2
        low(half_up, 0)
        take(2 * STEPS - 1, 1, 0)
        meet(NKEYS - 1, 1)
        low_gated(0, 0)
        low_gated(1, 1)
        low(half_up, 1)
        low_gated(2, 0)
        with dve.Fori(1, NKEYS // 2 - 1) as it:
            for u in range(2):
                low(it + half_up, u)
                low_gated(it * 2 + (u + 1), (u + 1) % 2)
        low(2 * half_up - 1, 0)
        low_gated(NKEYS - 1, 1)
        low(2 * half_up - 1, 1)

        dve.wait_ge(s_res2, 16)
        dve.wait_ge(s_fg, 16)
        dve.wait_ge(piece_used, 8 * NKEYS)
        for t in range(TT):
            for w in range(4):
                part = res2[:, t, w * 512:(w + 1) * 512]
                v_.tensor_tensor(part, part, ps[:, 4 * t + w, :], ALU.add).then_inc(h3_ready, 1)
        for t in range(TT):
            dve.wait_ge(ssq4, t + 1)
            v_.tensor_scalar(small[:, 6 + t:7 + t], small[:, 6 + t:7 + t], 1.0 / D, RMS_EPS, ALU.mult, ALU.add).then_inc(var4, 1)
            dve.wait_ge(std4, t + 1)
            v_.reciprocal(small[:, 6 + t:7 + t], small[:, 6 + t:7 + t]).then_inc(rs4, 1)
            dve.wait_ge(rs4, t + 1)
            v_.scalar_tensor_tensor(out=outb[:, t, :], in0=res2[:, t, :], scalar=small[:, 6 + t:7 + t], in1=fg[:],
                                    op0=ALU.mult, op1=ALU.mult).then_inc(fin, 1)

    ctx.close()


def kernel(**inputs):
    import numpy as np
    import concourse.bacc as bacc
    from concourse.bass_utils import run_bass_kernel_spmd

    a = {k: np.asarray(v) for k, v in inputs.items()}

    def columns(v, n):
        return v.reshape(n, P).T

    def stationary(w):
        rows, cols = w.shape
        w = w.reshape(rows // (8 * P), 8, P, cols // P, P).transpose(3, 0, 2, 1, 4)
        return w.reshape(-1, P, CHUNK)

    h = np.concatenate([a["meta_tokens"], a["x"][0]], axis=0)
    w_in = a["w_in"][0]
    conv = w_in[:, W:].reshape(D, 2, CT, P).transpose(0, 2, 1, 3).reshape(D, 2 * W)
    w_in = np.concatenate([conv, w_in[:, :W]], axis=1)
    pool_w = a["pool_w"][0].reshape(2, 2, 2, P, 2, P).transpose(0, 3, 1, 4, 2, 5).reshape(2, P, CHUNK)
    w_out = a["w_out"][0].reshape(2, CT, P, 2, CHUNK)[::-1].transpose(3, 0, 1, 2, 4).reshape(-1, P, CHUNK)
    front = np.concatenate([stationary(w_in), stationary(a["conv_pw_w"][0]), pool_w, w_out, stationary(a["peer_wq"][0])])
    assert front.shape[0] == FRONT
    dw = a["conv_dw_w"][0].reshape(TAPS, CT, P).transpose(2, 1, 0).reshape(P, CT * TAPS)
    vec = np.concatenate([
        columns(a["mix_norm_g"][0], KD), columns(a["pool_scale"][0], CT), dw, columns(a["conv_dw_b"][0], CT),
        columns(a["conv_ln_g"][0], CT), columns(a["conv_ln_b"][0], CT), columns(a["conv_pw_b"][0], CT),
        columns(a["ffn_norm_g"][0], KD)], axis=1)
    arrays = {
        "hT": h.T.reshape(KD, P, T).transpose(1, 0, 2),
        "x": a["x"][0].reshape(TT, P, D).transpose(1, 0, 2),
        "front": front,
        "down": a["peer_down"][0].reshape(NKEYS, P, 2, 8, P).transpose(0, 2, 4, 3, 1).reshape(2 * NKEYS, P, CHUNK),
        "up": a["peer_up"][0].reshape(NKEYS, P, 2, CHUNK).transpose(0, 2, 1, 3).reshape(2 * NKEYS, P, CHUNK),
        "keys": a["peer_keys"][0].transpose(3, 0, 1, 2).reshape(P, 2 * HEADS, NKEYS),
        "vec": vec,
        "fg": np.broadcast_to(a["final_norm_g"], (P, D)),
    }
    arrays = {f"in_{k}": np.ascontiguousarray(v) for k, v in arrays.items()}
    nc = bacc.Bacc("TRN2", target_bir_lowering=False, num_devices=1)
    aps = [nc.dram_tensor(k, v.shape, mybir.dt.from_np(v.dtype), kind="ExternalInput").ap() for k, v in arrays.items()]
    out = nc.dram_tensor("out", (TT, P, D), F32, kind="ExternalOutput").ap()
    bass_hymba_peer_block(nc, *aps, out)
    r = run_bass_kernel_spmd(nc, [arrays], core_ids=[0])
    return r.results[0]["out"].reshape(1, SEQ, D)
```

```python
from contextlib import ExitStack

import concourse.bass as bass
from concourse import mybir

P = 128
F32 = mybir.dt.float32
F32R = mybir.dt.float32r
BF16 = mybir.dt.bfloat16
U32 = mybir.dt.uint32
ALU = mybir.AluOpType
ACT = mybir.ActivationFunctionType
AX = mybir.AxisListType

D = 2048
KD = D // P
META, SEQ = 16, 256
T = META + SEQ
TT = SEQ // P
W = 1024
CT = W // P
TAPS = 31
PAD = TAPS - 1 - META
WINDOWS = (2, 4, 8, 16)
HEADS, TOPK, NKEYS = 8, 16, 128
SLOTS = HEADS * TOPK
RMS_EPS, LN_EPS = 1e-6, 1e-5
LOWEST = -3.4028235e38

CHUNK = 1024
PROJ_TILES = 3 * CT
C_CONV = 4 * CT
C_PROJ = 2 * PROJ_TILES
C_PW = CT
C_POOL = 2
C_OUT = 2 * KD
C_WQ = 2 * KD
FRONT = C_PROJ + C_PW + C_POOL + C_OUT + C_WQ
RAW = 4
PIECE = CHUNK // 2
SPLIT = 8
Q_PW = 2 * (C_PROJ - C_CONV)
Q_POOL = Q_PW + 2 * C_PW
Q_OUT = Q_POOL + 2 * C_POOL
Q_WQ = Q_OUT + 2 * C_OUT
Q_DOWN = Q_WQ + 2 * C_WQ
PIECES_WQ = 2 * C_WQ
UP0 = FRONT + 2 * NKEYS
HALF = NKEYS // 2
TOK = 4
PARTS = 3
PLAIN_TILES = 32
ROUTE_TILE = 24
CONV_OPS = TAPS + 1
RANK_OPS = 32
RANK_READ = (6, 16)
TAIL_OPS = 19
STEPS = SEQ // TOK

V_MIX, V_PS, V_DW, V_DB, V_LG, V_LB, V_PB, V_FFN = 0, 16, 24, 272, 280, 288, 296, 304
V_COLS = 320


def bass_hymba_peer_block(nc, hT_d, x_d, front_d, down_d, up_d, keys_d, vec_d, fg_d, out_d):
    spill_d = nc.dram_tensor("residual", (P, TT, D), F32, kind="Internal").ap()
    base = nc.sbuf_base + (-nc.sbuf_base) % 64
    top = [base]

    def at(name, shape, dt, offset):
        return nc.alloc_sbuf_tensor_at(name, shape, dt, offset=offset)

    def place(name, shape, dt):
        n = 2 if dt == BF16 else 4
        for s in shape[1:]:
            n *= s
        offset = top[0]
        top[0] += n + (-n) % 32
        return at(name, shape, dt, offset), offset

    gated, o_gated = place("gated", [P, NKEYS, SEQ], F32)
    raw, o_raw = place("raw", [P, RAW, CHUNK], F32)
    wh, _ = place("wh", [P, SPLIT, PIECE], F32R)
    wl, _ = place("wl", [P, SPLIT, PIECE], F32R)
    xh, o_xh = place("xh", [P, KD, SEQ], F32R)
    xl, o_xl = place("xl", [P, KD, SEQ], F32R)
    one_j, o_one = place("one_j", [P, 2, P, TOK], BF16)
    one_i, _ = place("one_i", [P, 2, HALF, TOK], BF16)
    gate_i, _ = place("gate_i", [P, 2, PARTS, HALF, TOK], BF16)
    gelu, o_gelu = place("gelu", [P, 2, SEQ], F32)
    slot_key, _ = place("slot_key", [P, 2, SEQ], BF16)
    slot_gate, _ = place("slot_gate", [P, PARTS, SEQ], BF16)
    small, _ = place("small", [P, 16], F32)
    ident, _ = place("ident", [P, P], F32)
    iota, _ = place("iota", [P, P], F32)
    iota_tok, _ = place("iota_tok", [P, P, TOK], BF16)
    assert top[0] <= nc.sbuf_usable_end, (top[0], nc.sbuf_usable_end)
    hnh = at("hnh", [P, KD, T], F32R, o_xh)
    hnl = at("hnl", [P, KD, T], F32R, o_xh + 4 * KD * T)
    ah = at("ah", [P, 2, SEQ], F32R, o_one)
    al = at("al", [P, 2, SEQ], F32R, o_one + 2048)
    gate_left = at("gate_left", [P, SEQ], F32, o_gelu)

    def early(name, shape, offset, dt=F32):
        return at(name, shape, dt, o_gated + offset)

    hn = early("hn", [P, KD, T], 0)
    glu = early("glu", [P, CT, PAD + T], 17408)
    cv = early("cv", [P, CT, SEQ], 26624)
    xp = early("xp", [P, CT, T], 34816)
    sum_a = early("sum_a", [P, CT, T], 43520)
    sum_b = early("sum_b", [P, CT, T], 52224)
    sig = early("sig", [P, 2, T], 60928)
    odd = early("odd", [P, SEQ], 63232)
    pooled = early("pooled", [P, CT, SEQ], 65536)
    pooled_l = early("pooled_l", [P, CT, SEQ], 65536, F32R)
    cv_sq = early("cv_sq", [P, CT, SEQ], 73728)
    act_cv = early("act_cv", [P, CT, SEQ], 90112)
    act_l = early("act_l", [P, CT, SEQ], 90112, F32R)
    act_h = early("act_h", [P, CT, SEQ], 0, F32R)
    pooled_h = early("pooled_h", [P, CT, SEQ], 8192, F32R)
    res = early("res", [P, TT, D], 98304)
    sq = early("sq", [P, 2, T], 114688)
    rstd1 = early("rstd1", [P, T], 116864)
    rstd2 = early("rstd2", [P, SEQ], 118016)
    vec = early("vec", [P, V_COLS], 119040)
    ones = early("ones", [P, P], 120320)
    junk = early("junk", [P, D], 120832)
    xn = early("xn", [P, TT, D], 0)
    keys = early("keys", [P, 2 * HEADS, NKEYS], 65536)
    qT = early("qT", [P, 2, SEQ], 73728)
    sv = early("sv", [P, TT, HEADS, 2, TOPK], 75776)
    si_u = early("si_u", [P, TT, HEADS, 2, TOPK], 77824, U32)
    si = early("si", [P, TT, HEADS, 2, TOPK], 79872)
    left = early("left", [P, TT, NKEYS], 81920)
    cand = early("cand", [P, TT, TOPK * TOPK], 82944)
    cand_left = early("cand_left", [P, TT, TOPK * TOPK], 84992)
    topv = early("topv", [P, TT, HEADS, TOPK], 87040)
    pos = early("pos", [P, TT, HEADS, TOPK], 88064, U32)
    pos_u = early("pos_u", [P, 2, TT * SLOTS], 89088, U32)
    pos_f = early("pos_f", [P, 2, TT * SLOTS], 91136)
    route = early("route", [P, 3, TT, SLOTS], 93184)
    norm = early("norm", [P, 2, TT * HEADS], 96256)
    match = early("match", [P, SLOTS, TOPK], 120832)
    res2 = at("res2", [P, TT, D], F32, o_xl)
    fg = at("fg", [P, D], F32, o_xh)
    junk2 = at("junk2", [P, D], F32, o_xh + 8192)
    outb = at("outb", [P, TT, D], F32, o_raw)

    ctx = ExitStack()
    ps = ctx.enter_context(nc.psum_tensor("ps", [P, 8, 512], F32))

    def sem(name):
        return ctx.enter_context(nc.semaphore(name))

    s_hT = [sem(f"hT_loaded{g}") for g in range(4)]
    s_raw = [sem(f"raw_loaded{s}") for s in range(RAW)]
    s_vec, s_x, s_keys, s_fg, s_res2 = sem("vec_loaded"), sem("x_loaded"), sem("keys_loaded"), sem("fg_loaded"), sem("res2_loaded")
    s_spill, s_out = sem("residual_spilled"), sem("out_stored")
    ones_ready, iota_ready, pad_ready, ident_ready = sem("ones_ready"), sem("iota_ready"), sem("pad_ready"), sem("ident_ready")
    front_used, wh_ready, wl_ready, wq_low_ready, piece_used = (
        sem("front_used"), sem("wh_ready"), sem("wl_ready"), sem("wq_low_ready"), sem("piece_used"))
    hnh_ready, hnl_ready = sem("hnh_ready"), sem("hnl_ready")
    act_h_ready, act_l_ready, pooled_h_ready, pooled_l_ready = (
        sem("act_h_ready"), sem("act_l_ready"), sem("pooled_h_ready"), sem("pooled_l_ready"))
    sq_ready, sq_used, var1, std1, rs1, hn_ready = sem("sq_ready"), sem("sq_used"), sem("var1"), sem("std1"), sem("rs1"), sem("hn_ready")
    sig_ready, glu_ready, tap_done = sem("sig_ready"), sem("glu_ready"), sem("tap_done")
    mean_done, xc_ready, cvsq_ready, var_done = sem("mean_done"), sem("xc_ready"), sem("cvsq_ready"), sem("var_done")
    var2, std2, rs2, ln_ready, silu_ready = sem("var2"), sem("std2"), sem("rs2"), sem("ln_ready"), sem("silu_ready")
    xp_ready, pool_step, pooled_ready = sem("xp_ready"), sem("pool_step"), sem("pooled_ready")
    yh_ready, yl_ready, res_ready = sem("yh_ready"), sem("yl_ready"), sem("res_ready")
    ssq3, var3, std3, rs3, xn_ready = sem("ssq3"), sem("var3"), sem("std3"), sem("rs3"), sem("xn_ready")
    xT_ps, xh_ready, xl_ready = sem("xT_ps"), sem("xh_ready"), sem("xl_ready")
    q_ready, score_done, rank = sem("q_ready"), sem("score_done"), sem("rank")
    z_ready, e_ready, tail, route_ps, slot_ready = sem("z_ready"), sem("e_ready"), sem("tail"), sem("route_ps"), sem("slot_ready")
    gelu_ready, tile_ready = sem("gelu_ready"), sem("tile_ready")
    eq_ready, onehot_ready, g_done, g_read = sem("eq_ready"), sem("onehot_ready"), sem("g_done"), sem("g_read")
    ah_ready, al_ready = sem("ah_ready"), sem("al_ready")
    h3_ready, ssq4, var4, std4, rs4, fin = sem("h3_ready"), sem("ssq4"), sem("var4"), sem("std4"), sem("rs4"), sem("fin")
    block = ctx.enter_context(nc.Block())

    def chunk(table, index):
        return table[bass.ds(index, 1)].rearrange("a p f -> (a p) f")

    def loads(c):
        return 16 * (c // RAW + 1)

    def gated_tile(i):
        return gated[:, bass.ds(i, 1), :].rearrange("p a t -> p (a t)")

    def bcast(ap, count):
        return ap.rearrange("p (n o) -> p n o", o=1).broadcast_to((P, ap.shape[1], count))

    def raw_piece(q):
        c = C_CONV + q // 2
        return raw[:, c % RAW, q % 2 * PIECE:(q % 2 + 1) * PIECE]

    def low_piece(q):
        return wl[:, q % SPLIT, :], raw_piece(q), wh[:, q % SPLIT, :].bitcast(F32)

    @block.sync
    def _(sp):
        for g in range(4):
            sp.dma_start(hn[:, 4 * g:4 * g + 4, :], hT_d[:, 4 * g:4 * g + 4, :]).then_inc(s_hT[g], 16)
            if g == 0:
                sp.dma_start(vec[:], vec_d).then_inc(s_vec, 16)
        for c in range(RAW):
            sp.dma_start(raw[:, c, :], chunk(front_d, c)).then_inc(s_raw[c], 16)
        sp.dma_start(res[:], x_d).then_inc(s_x, 16)
        with sp.Fori(1, C_CONV // RAW + 1) as it:
            for u in range(RAW):
                sp.wait_ge(front_used, it * RAW + (u + 1 - RAW))
                sp.dma_start(raw[:, u, :], chunk(front_d, it * RAW + u)).then_inc(s_raw[u], 16)

        def after_split(c, it=0):
            q = 2 * (c - RAW - C_CONV) + 2
            sp.wait_ge(wl_ready, it * (2 * RAW) + (q if q <= Q_WQ else q - PIECES_WQ))

        first = C_CONV + RAW
        with sp.Fori(0, (FRONT - C_WQ - first) // RAW) as it:
            for u in range(RAW):
                after_split(first + u, it)
                sp.dma_start(raw[:, u, :], chunk(front_d, it * RAW + (first + u))).then_inc(s_raw[u], 16)
        sp.wait_ge(piece_used, Q_OUT)
        sp.dma_start(keys[:], keys_d).then_inc(s_keys, 16)
        for c in range(first + (FRONT - C_WQ - first) // RAW * RAW, FRONT - C_WQ + RAW):
            after_split(c)
            sp.dma_start(raw[:, c % RAW, :], chunk(front_d, c)).then_inc(s_raw[c % RAW], 16)
        with sp.Fori(1, C_WQ // RAW) as it:
            for u in range(RAW):
                c = FRONT - C_WQ + u
                sp.wait_ge(wq_low_ready, it * (2 * RAW) + (2 * (u - RAW) + 2))
                sp.dma_start(raw[:, c % RAW, :], chunk(front_d, it * RAW + c)).then_inc(s_raw[c % RAW], 16)
        for u in range(RAW):
            sp.wait_ge(wq_low_ready, PIECES_WQ + 2 * (u - RAW) + 2)
            sp.dma_start(raw[:, (FRONT + u) % RAW, :], chunk(down_d, u)).then_inc(s_raw[(FRONT + u) % RAW], 16)
        for table, begin, skip in ((down_d, FRONT, 1), (up_d, UP0, 0)):
            with sp.Fori(skip, 2 * NKEYS // RAW) as it:
                for u in range(RAW):
                    after_split(begin + u + (RAW if skip else 0), it - 1 if skip else it)
                    slot = (begin + u) % RAW
                    sp.dma_start(raw[:, slot, :], chunk(table, it * RAW + u)).then_inc(s_raw[slot], 16)
        for t in range(TT):
            sp.wait_ge(fin, t + 1)
            sp.dma_start(out_d[t], outb[:, t, :]).then_inc(s_out, 16)
        sp.wait_ge(s_out, 16 * TT)

    @block.gpsimd
    def _(pool):
        nc.gpsimd.memset(ones[:], 1.0).then_inc(ones_ready, 1)
        nc.gpsimd.memset(glu[:, :, 0:PAD], 0.0).then_inc(pad_ready, 1)
        nc.gpsimd.iota(iota[:], [[1, P]], base=0, channel_multiplier=0,
                       allow_small_or_imprecise_dtypes=True).then_inc(iota_ready, 1)
        nc.gpsimd.iota(small[:, 0:1], [[0, 1]], base=0, channel_multiplier=1,
                       allow_small_or_imprecise_dtypes=True).then_inc(iota_ready, 1)
        for k in range(KD):
            pool.wait_ge(hnh_ready, k + 1)
            nc.gpsimd.tensor_tensor(hnl[:, k, :], hn[:, k, :], hnh[:, k, :].bitcast(F32), ALU.subtract).then_inc(hnl_ready, 1)
        step = 0
        for g, window in enumerate(WINDOWS):
            tiles = slice(2 * g, 2 * g + 2)
            pool.wait_ge(xp_ready, 2 * g + 2)
            src, span = xp, 1
            while span < window:
                dst = sum_b if src is sum_a else sum_a
                lo = 2 * span - 1
                nc.gpsimd.tensor_tensor(dst[:, tiles, lo:T], src[:, tiles, lo:T], src[:, tiles, lo - span:T - span],
                                        ALU.add).then_inc(pool_step, 1)
                step += 1
                pool.wait_ge(pool_step, step)
                src, span = dst, 2 * span
            dst = sum_b if src is sum_a else sum_a
            nc.gpsimd.tensor_scalar(dst[:, tiles, META:T], src[:, tiles, META:T], 1.0 / window, None,
                                    ALU.mult).then_inc(pool_step, 1)
            step += 1
            pool.wait_ge(pool_step, step)
            nc.gpsimd.tensor_tensor(pooled[:, tiles, :], dst[:, tiles, META:T], xp[:, tiles, META:T],
                                    ALU.subtract).then_inc(pooled_ready, 1)
        with pool.Fori(0, 2 * HEADS // 2) as it:
            for u in range(2):
                for part in range(4):
                    q = Q_WQ + 4 * u + part
                    pool.wait_ge(wh_ready, it * 8 + (q + 1))
                    nc.gpsimd.tensor_tensor(*low_piece(q), ALU.subtract).then_inc(wq_low_ready, 1)

    @block.scalar
    def _(act):
        for k in range(KD):
            if k % 4 == 0:
                act.wait_ge(s_hT[k // 4], 16)
            if k >= 2:
                act.wait_ge(sq_used, k - 1)
            nc.scalar.activation(sq[:, k % 2, :], hn[:, k, :], ACT.Square).then_inc(sq_ready, 1)
        act.wait_ge(var1, 1)
        nc.scalar.activation(rstd1[:], rstd1[:], ACT.Sqrt).then_inc(std1, 1)

        for k in range(KD):
            act.wait_ge(hn_ready, k + 1)
            nc.scalar.activation(hnh[:, k, :], hn[:, k, :], ACT.Copy).then_inc(hnh_ready, 1)

        def glu_gate(c, u):
            act.wait_ge(front_used, c * 4 + 4)
            nc.scalar.activation(sig[:, u, :], ps[:, 2 * u + 1, 0:T], ACT.Sigmoid).then_inc(sig_ready, 1)

        def high(q, count, it=0):
            for n in range(q, q + count):
                c = C_CONV + n // 2
                if n % 2 == 0:
                    act.wait_ge(s_raw[c % RAW], it * 16 + loads(c))
                if n >= SPLIT:
                    act.wait_ge(piece_used, it * 8 + (n - SPLIT + 1))
                nc.scalar.activation(wh[:, n % SPLIT, :], raw_piece(n), ACT.Copy).then_inc(wh_ready, 1)

        for u in range(2):
            glu_gate(u, u)
        with act.Fori(1, CT // 2 - 1) as it:
            for u in range(2):
                act.wait_ge(glu_ready, it * 2 + (u - 1))
                glu_gate(it * 2 + u, u)
        for u in range(2):
            act.wait_ge(glu_ready, CT - 3 + u)
            glu_gate(CT - 2 + u, u)
            high(4 * u, 4)

        def keep_xp(n):
            act.wait_ge(piece_used, 4 * (n + 1))
            nc.scalar.activation(xp[:, n, :], ps[:, n % 4, 0:T], ACT.Copy).then_inc(xp_ready, 1)

        for n in range(2):
            keep_xp(n)
            high(4 * (n + 2), 4)
        act.wait_ge(xc_ready, 1)
        nc.scalar.activation(cv_sq[:], cv[:], ACT.Square).then_inc(cvsq_ready, 1)
        for n in range(2, 5):
            keep_xp(n)
            high(4 * (n + 2), 4)
        act.wait_ge(var2, 1)
        nc.scalar.activation(rstd2[:], rstd2[:], ACT.Sqrt).then_inc(std2, 1)
        keep_xp(5)
        high(4 * 7, 4)
        act.wait_ge(ln_ready, 1)
        for k in range(CT):
            nc.scalar.activation(act_cv[:, k, :], cv[:, k, :], ACT.Silu, bias=vec[:, V_LB + k:V_LB + k + 1],
                                 scale=vec[:, V_LG + k:V_LG + k + 1]).then_inc(silu_ready, 1)
        keep_xp(6)
        act.wait_ge(silu_ready, CT)
        for k in range(CT):
            nc.scalar.activation(act_h[:, k, :], act_cv[:, k, :], ACT.Copy).then_inc(act_h_ready, 1)
        high(Q_PW, 4)
        keep_xp(7)
        high(Q_PW + 4, 4)

        for m in range(CT):
            act.wait_ge(piece_used, Q_PW + 2 * m + 2)
            nc.scalar.activation(xh[:, CT + m, :], ps[:, m % 4, 0:SEQ], ACT.Identity,
                                 bias=vec[:, V_PB + m:V_PB + m + 1]).then_inc(yh_ready, 1)
            high(Q_PW + 8 + 2 * m, 2)
            if m % 2:
                g = m // 2
                act.wait_ge(pooled_ready, g + 1)
                nc.scalar.activation(pooled_h[:, 2 * g:2 * g + 2, :], pooled[:, 2 * g:2 * g + 2, :],
                                     ACT.Copy).then_inc(pooled_h_ready, 1)
        for m in range(CT):
            act.wait_ge(piece_used, Q_POOL + m // 2 + 1)
            nc.scalar.activation(xh[:, m, :], ps[:, m % 4, 0:SEQ], ACT.Copy,
                                 scale=vec[:, V_PS + m:V_PS + m + 1]).then_inc(yh_ready, 1)
        high(Q_OUT + 4, 4)
        with act.Fori(1, 2 * C_OUT // 8) as it:
            high(Q_OUT, 8, it)
        high(Q_WQ, 8)
        for t in range(TT):
            act.wait_ge(res_ready, 4 + 2 * t + 2)
            if t:
                act.wait_ge(ssq3, t)
            nc.scalar.activation(junk[:], res[:, t, :], ACT.Square, accum_out=small[:, 2 + t:3 + t]).then_inc(ssq3, 1)
        act.wait_ge(var3, 1)
        nc.scalar.activation(small[:, 2:4], small[:, 2:4], ACT.Sqrt).then_inc(std3, 1)
        act.dma_start(spill_d, res[:]).then_inc(s_spill, 16)
        for k in range(KD):
            act.wait_ge(xT_ps, k + 1)
            nc.scalar.activation(xh[:, k, :], ps[:, k % 8, 0:SEQ], ACT.Copy,
                                 scale=vec[:, V_FFN + k:V_FFN + k + 1]).then_inc(xh_ready, 1)

        def query(n, u):
            act.wait_ge(piece_used, n * 4 + (Q_WQ + 4))
            nc.scalar.activation(qT[:, u, :], ps[:, u, 0:SEQ], ACT.Copy).then_inc(q_ready, 1)

        for u in range(2):
            query(u, u)
            high(Q_WQ + 8 + 4 * u, 4)
        with act.Fori(1, HEADS) as it:
            for u in range(2):
                act.wait_ge(score_done, it * 2 + (u - 1))
                query(it * 2 + u, u)
                high(Q_WQ + 8 + 4 * u, 4, it)

        def gelu_into(out, i, u):
            act.wait_ge(piece_used, i * 4 + (Q_DOWN + 4))
            nc.scalar.activation(out, ps[:, u, 0:SEQ], ACT.Gelu).then_inc(gelu_ready, 1)

        act.wait_ge(z_ready, 1)
        nc.scalar.activation(route[:, 2], route[:, 2], ACT.Exp).then_inc(e_ready, 1)
        act.wait_ge(s_spill, 16)

        def direct_tiles(lo, hi):
            with act.Fori(lo // 2, hi // 2) as it:
                for u in range(2):
                    gelu_into(gated_tile(it * 2 + u), it * 2 + u, u)
                    high(Q_DOWN + 8 + 4 * u, 4, it)

        direct_tiles(0, ROUTE_TILE)
        act.wait_ge(route_ps, 1)
        for r in range(2):
            nc.scalar.activation(slot_key[:, r, :], ps[:, 4 + r, 0:SEQ], ACT.Copy).then_inc(slot_ready, 1)
        nc.scalar.activation(slot_gate[:, 0, :], ps[:, 6, 0:SEQ], ACT.Copy).then_inc(slot_ready, 1)
        direct_tiles(ROUTE_TILE, HALF)
        for i in (HALF, HALF + 1):
            gelu_into(gelu[:, i % 2, :], i, i % 2)
            high(Q_DOWN + 8 + 4 * (i % 2), 4, HALF // 2)
        with act.Fori(HALF // 2 + 1, NKEYS // 2) as it:
            for u in range(2):
                act.wait_ge(tile_ready, it * 2 + (u - HALF - 1))
                gelu_into(gelu[:, u, :], it * 2 + u, u)
                high(Q_DOWN + 8 + 4 * u, 4, it)

        def high_gated(i, u):
            nc.scalar.activation(ah[:, u, :], gated_tile(i), ACT.Copy).then_inc(ah_ready, 1)

        act.dma_start(res2[:], spill_d).then_inc(s_res2, 16)
        act.dma_start(fg[:], fg_d).then_inc(s_fg, 16)
        act.wait_ge(g_read, 2 * STEPS)
        for i in range(2):
            high_gated(i, i)
        act.wait_ge(tile_ready, NKEYS - HALF)
        q_up = Q_DOWN + 4 * NKEYS
        with act.Fori(0, NKEYS // 2 - 1) as it:
            for u in range(2):
                high(q_up + 8 + 4 * u, 4, it)
                high_gated(it * 2 + (u + 2), u)
        for t in range(TT):
            act.wait_ge(h3_ready, 4 * t + 4)
            if t:
                act.wait_ge(ssq4, t)
            nc.scalar.activation(junk2[:], res2[:, t, :], ACT.Square, accum_out=small[:, 6 + t:7 + t]).then_inc(ssq4, 1)
            act.wait_ge(var4, t + 1)
            nc.scalar.activation(small[:, 6 + t:7 + t], small[:, 6 + t:7 + t], ACT.Sqrt).then_inc(std4, 1)

    @block.tensor
    def _(pe):
        matmul = nc.tensor.matmul
        pe.wait_ge(ones_ready, 1)
        for k in range(KD):
            pe.wait_ge(sq_ready, k + 1)
            matmul(ps[:, 4, 0:T], ones[:], sq[:, k % 2, :], start=(k == 0), stop=(k == KD - 1)).then_inc(sq_used, 1)

        def proj_tile(it, u, first=False):
            for half in range(2):
                c = 2 * u + half
                pe.wait_ge(s_raw[c % RAW], it * 32 + loads(c))
                for k in range(8):
                    kk = 8 * half + k
                    if first:
                        pe.wait_ge(hn_ready, kk + 1)
                    m = matmul(ps[:, u, 0:T], raw[:, c % RAW, k * P:(k + 1) * P], hn[:, kk, :],
                               start=(kk == 0), stop=(kk == KD - 1))
                m.then_inc(front_used, 1)

        for u in range(4):
            proj_tile(0, u, first=(u == 0))
        with pe.Fori(1, 2 * CT // 4) as it:
            for u in range(4):
                if u % 2 == 0:
                    pe.wait_ge(glu_ready, it * 2 + (u // 2 - 1))
                proj_tile(it, u)

        def split_products(out, weights, high_x, low_x, start, stop, swap=False):
            slot, cols = weights
            w_h, w_l = wh[:, slot, cols], wl[:, slot, cols]
            for a, b, begin, end in ((w_h, high_x, start, False), (w_h, low_x, False, False), (w_l, high_x, False, stop)):
                m = matmul(out, b, a, start=begin, stop=end) if swap else matmul(out, a, b, start=begin, stop=end)
            return m

        def piece_ready(q, it=0):
            if Q_WQ <= q < Q_DOWN:
                pe.wait_ge(wq_low_ready, it * 8 + (q - Q_WQ + 1))
            else:
                pe.wait_ge(wl_ready, it * 8 + (q + 1 - (PIECES_WQ if q >= Q_DOWN else 0)))

        def block_cols(k):
            return slice(k * P, (k + 1) * P)

        def pool_tile(n):
            if n < 4:
                pe.wait_ge(glu_ready, CT - 1 + n // 2)
            else:
                pe.wait_ge(xp_ready, n - 3)
            for part in range(4):
                q = 4 * n + part
                piece_ready(q)
                for k in range(4):
                    kk = 4 * part + k
                    if n == 0:
                        pe.wait_ge(hnl_ready, kk + 1)
                    m = split_products(ps[:, n % 4, 0:T], (q % SPLIT, block_cols(k)), hnh[:, kk, :], hnl[:, kk, :],
                                       kk == 0, kk == KD - 1)
                m.then_inc(piece_used, 1)

        for n in range(3):
            pool_tile(n)
        for k in range(CT):
            pe.wait_ge(tap_done, CONV_OPS * (k + 1))
            m = matmul(ps[:, 5, 0:SEQ], ones[:], cv[:, k, :], start=(k == 0), stop=(k == CT - 1))
        m.then_inc(mean_done, 1)
        for n in range(3, 5):
            pool_tile(n)
        pe.wait_ge(cvsq_ready, 1)
        for k in range(CT):
            m = matmul(ps[:, 6, 0:SEQ], ones[:], cv_sq[:, k, :], start=(k == 0), stop=(k == CT - 1))
        m.then_inc(var_done, 1)
        for n in range(5, 8):
            pool_tile(n)

        for m in range(CT):
            if m < 4:
                pe.wait_ge(xp_ready, 5 + m)
            else:
                pe.wait_ge(yl_ready, m - 3)
            for part in range(2):
                q = Q_PW + 2 * m + part
                piece_ready(q)
                for k in range(4):
                    kk = 4 * part + k
                    if m == 0:
                        pe.wait_ge(act_l_ready, kk + 1)
                    last = split_products(ps[:, m % 4, 0:SEQ], (q % SPLIT, block_cols(k)), act_h[:, kk, :],
                                          act_l[:, kk, :], kk == 0, kk == CT - 1)
                last.then_inc(piece_used, 1)
        for g in range(len(WINDOWS)):
            q = Q_POOL + g
            piece_ready(q)
            pe.wait_ge(pooled_l_ready, g + 1)
            for d in range(2):
                m = 2 * g + d
                pe.wait_ge(yl_ready, CT + m - 3)
                for k in range(2):
                    last = split_products(ps[:, m % 4, 0:SEQ], (q % SPLIT, block_cols(2 * d + k)),
                                          pooled_h[:, 2 * g + k, :], pooled_l[:, 2 * g + k, :], k == 0, k == 1)
            last.then_inc(piece_used, 1)

        for half in range(2):
            for n in range(KD):
                k = (n + CT) % KD
                pe.wait_ge(yl_ready, n + 1 if half == 0 else KD)
                for w in range(2):
                    q = Q_OUT + 2 * (half * KD + n) + w
                    piece_ready(q)
                    for t in range(TT):
                        tok = slice(t * P, (t + 1) * P)
                        last = split_products(ps[:, 4 * (1 - half) + 2 * t + w, :], (q % SPLIT, slice(0, PIECE)),
                                              xh[:, k, tok], xl[:, k, tok], n == 0, n == KD - 1, swap=True)
                    last.then_inc(piece_used, 1)

        pe.wait_ge(ident_ready, 1)
        for k in range(KD):
            if k >= 8:
                pe.wait_ge(xl_ready, k - 7)
            for t in range(TT):
                pe.wait_ge(xn_ready, TT if k else t + 1)
                last = nc.tensor.transpose(ps[:, k % 8, t * P:(t + 1) * P], xn[:, t, k * P:(k + 1) * P], ident[:])
            last.then_inc(xT_ps, 1)

        def query(it, v, first=False):
            if not (first and v < 2):
                pe.wait_ge(q_ready, it * 4 + (v - 1))
            elif v == 0:
                pe.wait_ge(xl_ready, 10)
            for part in range(4):
                q = Q_WQ + 4 * v + part
                piece_ready(q, it * 2)
                for k in range(4):
                    kk = 4 * part + k
                    if first and v == 0:
                        pe.wait_ge(xl_ready, kk + 1)
                    m = split_products(ps[:, v % 2, 0:SEQ], (q % SPLIT, block_cols(k)), xh[:, kk, :], xl[:, kk, :],
                                       kk == 0, kk == KD - 1)
                m.then_inc(piece_used, 1)

        def scores(it, v, first=False):
            head, half = v // 2, v % 2
            pe.wait_ge(q_ready, it * 4 + (v + 1))
            if not first:
                pe.wait_ge(rank, it * (2 * RANK_OPS) + ((head - 2) * RANK_OPS + RANK_READ[half]))
            for t in range(TT):
                key = keys[:, bass.ds(it * 4 + v, 1), :].rearrange("p a n -> p (a n)")
                m = matmul(ps[:, 2 + v, t * P:(t + 1) * P], qT[:, half, t * P:(t + 1) * P], key, start=True, stop=True)
            m.then_inc(score_done, 1)

        query(0, 0, first=True)
        pe.wait_ge(s_keys, 16)
        for v in range(1, 4):
            query(0, v, first=True)
            scores(0, v - 1, first=True)

        def queries(it, first=False):
            query(it, 0)
            scores(it - 1, 3, first=first)
            for v in range(1, 4):
                query(it, v)
                scores(it, v - 1)

        queries(1, first=True)
        with pe.Fori(2, HEADS // 2) as it:
            queries(it)
        scores(HEADS // 2 - 1, 3)

        def down_tile(it, u, first=False, steps=()):
            if not first:
                pe.wait_ge(gelu_ready, it * 2 + (u - 1))
            for part in range(4):
                q = Q_DOWN + 4 * u + part
                piece_ready(q, it)
                for k in range(4):
                    kk = 4 * part + k
                    m = split_products(ps[:, u, 0:SEQ], (q % SPLIT, block_cols(k)), xh[:, kk, :], xl[:, kk, :],
                                       kk == 0, kk == KD - 1)
                m.then_inc(piece_used, 1)
                if part % 2 and part // 2 < len(steps):
                    gate_step(*steps[part // 2])

        def gate_step(s, slot, first=False):
            if not first:
                pe.wait_ge(g_read, s - 1)
            pe.wait_ge(onehot_ready, s + 1)
            for n, part in [(n, part) for n in range(TOK) for part in range(PARTS)]:
                m = matmul(ps[:, 2 + slot, n * HALF:(n + 1) * HALF], one_j[:, slot, :, n],
                           gate_i[:, slot, part, :, n], start=(part == 0), stop=(part == PARTS - 1))
            m.then_inc(g_done, 1)

        for u in range(2):
            pe.wait_ge(q_ready, 2 * HEADS - 1 + u)
            down_tile(0, u, first=True)
        with pe.Fori(1, ROUTE_TILE // 2) as it:
            for u in range(2):
                down_tile(it, u)
        pe.wait_ge(tail, TAIL_OPS)
        for r in range(3):
            for t in range(TT):
                m = nc.tensor.transpose(ps[:, 4 + r, t * P:(t + 1) * P], route[:, r, t, :], ident[:])
        m.then_inc(route_ps, 1)
        with pe.Fori(ROUTE_TILE // 2, PLAIN_TILES // 2) as it:
            for u in range(2):
                down_tile(it, u)
        down_tile(PLAIN_TILES // 2, 0, steps=((0, 0, True), (1, 1, True)))
        down_tile(PLAIN_TILES // 2, 1, steps=((2, 0), (3, 1)))
        with pe.Fori(PLAIN_TILES // 2 + 1, HALF // 2) as it:
            for u in range(2):
                down_tile(it, u, steps=[(it * 4 + (2 * u + v - 2 * PLAIN_TILES), v) for v in range(2)])
        with pe.Fori(HALF // 2, NKEYS // 2) as it:
            for u in range(2):
                down_tile(it, u, steps=[(it * 2 + u, u)])

        def up_tile(it, u, start=False, stop=False):
            pe.wait_ge(al_ready, it * 2 + (u + 1))
            for part in range(4):
                q = Q_DOWN + 4 * NKEYS + 4 * u + part
                piece_ready(q, it)
                for t in range(TT):
                    tok = slice(t * P, (t + 1) * P)
                    m = split_products(ps[:, 4 * t + part, :], (q % SPLIT, slice(0, PIECE)), ah[:, u, tok], al[:, u, tok],
                                       start, stop, swap=True)
                m.then_inc(piece_used, 1)

        pe.wait_ge(gelu_ready, NKEYS)
        pe.wait_ge(g_read, 2 * STEPS)
        up_tile(0, 0, start=True)
        up_tile(0, 1)
        with pe.Fori(1, NKEYS // 2 - 1) as it:
            for u in range(2):
                up_tile(it, u)
        up_tile(NKEYS // 2 - 1, 0)
        up_tile(NKEYS // 2 - 1, 1, stop=True)

    @block.vector
    def _(dve):
        v_ = nc.vector
        dve.wait_ge(iota_ready, 2)
        v_.tensor_scalar(ident[:], iota[:], small[:, 0:1], None, ALU.is_equal).then_inc(ident_ready, 1)
        v_.tensor_copy(iota_tok[:], bcast(iota[:], TOK)).then_inc(ident_ready, 1)
        dve.wait_ge(sq_used, KD)
        v_.tensor_scalar(rstd1[:], ps[:, 4, 0:T], 1.0 / D, RMS_EPS, ALU.mult, ALU.add).then_inc(var1, 1)
        dve.wait_ge(std1, 1)
        v_.reciprocal(rstd1[:], rstd1[:]).then_inc(rs1, 1)
        dve.wait_ge(s_vec, 16)
        dve.wait_ge(rs1, 1)
        for k in range(KD):
            v_.scalar_tensor_tensor(out=hn[:, k, :], in0=hn[:, k, :], scalar=vec[:, V_MIX + k:V_MIX + k + 1], in1=rstd1[:],
                                    op0=ALU.mult, op1=ALU.mult).then_inc(hn_ready, 1)

        def low(q, count=4, it=0):
            for n in range(q, q + count):
                dve.wait_ge(wh_ready, it * 8 + (n + 1))
                v_.tensor_tensor(*low_piece(n), ALU.subtract).then_inc(wl_ready, 1)

        def conv_tile(c, u, pieces=()):
            dve.wait_ge(sig_ready, c + 1)
            v_.tensor_tensor(glu[:, bass.ds(c, 1), PAD:PAD + T].rearrange("p a t -> p (a t)"), ps[:, 2 * u, 0:T],
                             sig[:, u, :], ALU.mult).then_inc(glu_ready, 1)
            dve.wait_ge(glu_ready, c + 1)
            acc = cv[:, bass.ds(c, 1), :].rearrange("p a t -> p (a t)")
            for j in range(TAPS):
                x = glu[:, bass.ds(c, 1), j:j + SEQ].rearrange("p a t -> p (a t)")
                w = vec[:, bass.ds(c * TAPS + (V_DW + j), 1)]
                if j in pieces:
                    low(pieces[j], 4)
                if j >= 2:
                    dve.wait_ge(tap_done, c * CONV_OPS + (j - 1))
                if j == 0:
                    ins = v_.tensor_scalar(acc, x, w, vec[:, bass.ds(c + V_DB, 1)], ALU.mult, ALU.add)
                elif j == 1:
                    ins = v_.tensor_scalar(odd[:], x, w, None, ALU.mult)
                else:
                    dst = odd[:] if j % 2 else acc
                    ins = v_.scalar_tensor_tensor(out=dst, in0=x, scalar=w, in1=dst, op0=ALU.mult, op1=ALU.add)
                ins.then_inc(tap_done, 1)
            dve.wait_ge(tap_done, c * CONV_OPS + TAPS)
            v_.tensor_tensor(acc, acc, odd[:], ALU.add).then_inc(tap_done, 1)
            dve.wait_ge(tap_done, c * CONV_OPS + CONV_OPS)

        dve.wait_ge(pad_ready, 1)
        with dve.Fori(0, CT // 2 - 1) as it:
            for u in range(2):
                conv_tile(it * 2 + u, u)
        conv_tile(CT - 2, 0)
        conv_tile(CT - 1, 1, pieces={2: 0, 10: 4, 24: 8})
        dve.wait_ge(mean_done, 1)
        mean = ps[:, 5:6, 0:SEQ].broadcast_to((P, CT, SEQ))
        v_.scalar_tensor_tensor(out=cv[:], in0=mean, scalar=-1.0 / W, in1=cv[:], op0=ALU.mult, op1=ALU.add).then_inc(xc_ready, 1)
        low(12, 8)
        dve.wait_ge(var_done, 1)
        v_.tensor_scalar(rstd2[:], ps[:, 6, 0:SEQ], 1.0 / W, LN_EPS, ALU.mult, ALU.add).then_inc(var2, 1)
        low(20, 4)
        dve.wait_ge(std2, 1)
        v_.reciprocal(rstd2[:], rstd2[:]).then_inc(rs2, 1)
        dve.wait_ge(rs2, 1)
        v_.tensor_tensor(cv[:], cv[:], rstd2[:].rearrange("p (a t) -> p a t", a=1).broadcast_to((P, CT, SEQ)),
                         ALU.mult).then_inc(ln_ready, 1)
        low(24, 8)
        for k in range(CT):
            dve.wait_ge(act_h_ready, k + 1)
            v_.tensor_tensor(act_l[:, k, :], act_cv[:, k, :], act_h[:, k, :].bitcast(F32), ALU.subtract).then_inc(act_l_ready, 1)
        low(Q_PW, 8)
        for m in range(CT):
            dve.wait_ge(yh_ready, m + 1)
            v_.scalar_tensor_tensor(out=xl[:, CT + m, :], in0=ps[:, m % 4, 0:SEQ], scalar=vec[:, V_PB + m:V_PB + m + 1],
                                    in1=xh[:, CT + m, :].bitcast(F32), op0=ALU.add, op1=ALU.subtract).then_inc(yl_ready, 1)
            low(Q_PW + 8 + 2 * m, 2)
            if m % 2:
                g = m // 2
                dve.wait_ge(pooled_h_ready, g + 1)
                v_.tensor_tensor(pooled_l[:, 2 * g:2 * g + 2, :], pooled[:, 2 * g:2 * g + 2, :],
                                 pooled_h[:, 2 * g:2 * g + 2, :].bitcast(F32), ALU.subtract).then_inc(pooled_l_ready, 1)
        for m in range(CT):
            dve.wait_ge(yh_ready, CT + m + 1)
            v_.scalar_tensor_tensor(out=xl[:, m, :], in0=ps[:, m % 4, 0:SEQ], scalar=vec[:, V_PS + m:V_PS + m + 1],
                                    in1=xh[:, m, :].bitcast(F32), op0=ALU.mult, op1=ALU.subtract).then_inc(yl_ready, 1)
        low(Q_OUT + 4, 4)
        with dve.Fori(1, 5) as it:
            low(Q_OUT, 8, it)
        dve.wait_ge(s_x, 16)

        def join(half):
            dve.wait_ge(piece_used, Q_OUT + (half + 1) * 2 * KD)
            for t in range(TT):
                for w in range(2):
                    part = res[:, t, half * 1024 + w * 512:half * 1024 + w * 512 + 512]
                    v_.tensor_tensor(part, part, ps[:, 4 * (1 - half) + 2 * t + w, :], ALU.add).then_inc(res_ready, 1)

        join(0)
        with dve.Fori(5, 2 * C_OUT // 8) as it:
            low(Q_OUT, 8, it)
        join(1)
        dve.wait_ge(ssq3, TT)
        v_.tensor_scalar(small[:, 2:4], small[:, 2:4], 1.0 / D, RMS_EPS, ALU.mult, ALU.add).then_inc(var3, 1)
        dve.wait_ge(std3, 1)
        v_.reciprocal(small[:, 2:4], small[:, 2:4]).then_inc(rs3, 1)
        dve.wait_ge(rs3, 1)
        for t in range(TT):
            v_.tensor_scalar(xn[:, t, :], res[:, t, :], small[:, 2 + t:3 + t], None, ALU.mult).then_inc(xn_ready, 1)

        for k in range(KD):
            dve.wait_ge(xh_ready, k + 1)
            v_.scalar_tensor_tensor(out=xl[:, k, :], in0=ps[:, k % 8, 0:SEQ], scalar=vec[:, V_FFN + k:V_FFN + k + 1],
                                    in1=xh[:, k, :].bitcast(F32), op0=ALU.mult, op1=ALU.subtract).then_inc(xl_ready, 1)

        done = [0]

        def ranked(ins):
            ins.then_inc(rank, 1)
            done[0] += 1
            if done[0] >= 2:
                dve.wait_ge(rank, done[0] - 1)

        def top16(values, indices, source, rest):
            for t in range(TT):
                ranked(v_.max(values(t)[:, 0:8], source(t)))
            for t in range(TT):
                ranked(v_.max_index(indices(t)[:, 0:8], values(t)[:, 0:8], source(t)))
            for t in range(TT):
                ranked(v_.match_replace(rest(t), values(t)[:, 0:8], source(t), LOWEST))
            for t in range(TT):
                ranked(v_.max(values(t)[:, 8:16], rest(t)))
            for t in range(TT):
                ranked(v_.max_index(indices(t)[:, 8:16], values(t)[:, 8:16], rest(t)))

        for h in range(HEADS):
            for half in range(2):
                dve.wait_ge(score_done, 2 * h + half + 1)
                top16(lambda t: sv[:, t, h, half, :], lambda t: si_u[:, t, h, half, :],
                      lambda t: ps[:, 2 + h % 2 * 2 + half, t * P:(t + 1) * P], lambda t: left[:, t, :])
            for t in range(TT):
                first = bcast(sv[:, t, h, 0, :], TOPK)
                second = sv[:, t, h, 1:2, :].broadcast_to((P, TOPK, TOPK))
                ranked(v_.tensor_tensor(cand[:, t, :].rearrange("p (a b) -> p a b", a=TOPK), first, second, ALU.add))
            top16(lambda t: topv[:, t, h, :], lambda t: pos[:, t, h, :], lambda t: cand[:, t, :], lambda t: cand_left[:, t, :])
            assert done[0] == RANK_OPS * (h + 1)
        dve.wait_ge(rank, RANK_OPS * HEADS)

        def down_low(it, u, parts=range(4)):
            for part in parts:
                low(Q_DOWN + 4 * u + part, 1, it)

        steps = [0]

        def tailed(ins):
            ins.then_inc(tail, 1)
            steps[0] += 1

        flat = "p t h k -> p (t h k)"
        top = topv[:].rearrange("p t h k -> p (t h) k")
        exp_ = route[:, 2].rearrange("p t (h k) -> p (t h) k", h=HEADS)
        v_.tensor_tensor(exp_, top, top[:, :, 0:1].broadcast_to((P, TT * HEADS, TOPK)), ALU.subtract).then_inc(z_ready, 1)
        down_low(0, 0)
        tailed(v_.tensor_copy(si[:].rearrange("p t h c k -> p (t h c k)"), si_u[:].rearrange("p t h c k -> p (t h c k)")))
        tailed(v_.tensor_scalar(pos_u[:, 0, :], pos[:].rearrange(flat), 4, None, ALU.logical_shift_right))
        tailed(v_.tensor_scalar(pos_u[:, 1, :], pos[:].rearrange(flat), TOPK - 1, None, ALU.bitwise_and))
        down_low(0, 1)
        dve.wait_ge(tail, 3)
        tailed(v_.tensor_copy(pos_f[:], pos_u[:]))
        dve.wait_ge(e_ready, 1)
        tailed(v_.tensor_reduce(norm[:, 0, :], exp_, AX.X, ALU.add))
        down_low(1, 0)
        dve.wait_ge(tail, 5)
        tailed(v_.reciprocal(norm[:, 1, :], norm[:, 0, :]))
        down_low(1, 1)
        dve.wait_ge(tail, 6)
        tailed(v_.tensor_tensor(exp_, exp_, bcast(norm[:, 1, :], TOPK), ALU.mult))
        tile = 4
        for r in range(2):
            for t in range(TT):
                down_low(tile // 2, 0)
                dve.wait_ge(tail, steps[0])
                tailed(v_.tensor_tensor(match[:], bcast(pos_f[:, r, t * SLOTS:(t + 1) * SLOTS], TOPK),
                                        iota[:, 0:TOPK].rearrange("p (a n) -> p a n", a=1).broadcast_to((P, SLOTS, TOPK)),
                                        ALU.is_equal))
                down_low(tile // 2, 1)
                dve.wait_ge(tail, steps[0])
                by_head = match[:].rearrange("p (h k) n -> p h k n", h=HEADS)
                index = si[:, t, :, r:r + 1, :].broadcast_to((P, HEADS, TOPK, TOPK))
                tailed(v_.tensor_tensor(by_head, by_head, index, ALU.mult))
                down_low(tile // 2 + 1, 0)
                dve.wait_ge(tail, steps[0])
                tailed(v_.tensor_reduce(route[:, r, t, :], match[:], AX.X, ALU.add))
                down_low(tile // 2 + 1, 1)
                tile += 4
        assert steps[0] == TAIL_OPS and tile == 20

        def plain(lo, hi):
            with dve.Fori(lo // 2, hi // 2) as it:
                for u in range(2):
                    down_low(it, u)

        def onehots(s, u, half, first=False):
            if not first:
                dve.wait_ge(g_done, s - 1)
            tok = bass.ds((s - (STEPS if half == 0 else 0)) * TOK, TOK)
            first_key, second_key = (slot_key[:, r:r + 1, tok] for r in range(2))
            v_.tensor_tensor(one_i[:, u], iota_tok[:, half * HALF:(half + 1) * HALF, :],
                             first_key.broadcast_to((P, HALF, TOK)), ALU.is_equal).then_inc(eq_ready, 1)
            v_.tensor_tensor(one_j[:, u], iota_tok[:], second_key.broadcast_to((P, P, TOK)), ALU.is_equal).then_inc(eq_ready, 1)
            dve.wait_ge(eq_ready, s * 2 + 2)
            v_.tensor_tensor(gate_i[:, u], one_i[:, u].rearrange("p (a i) t -> p a i t", a=1).broadcast_to((P, PARTS, HALF, TOK)),
                             slot_gate[:, :, tok].rearrange("p r (a t) -> p r a t", a=1).broadcast_to((P, PARTS, HALF, TOK)),
                             ALU.mult).then_inc(onehot_ready, 1)

        def take(s, u, half):
            dve.wait_ge(g_done, s + 1)
            dst = gated[:, half * HALF:(half + 1) * HALF, bass.ds((s - (STEPS if half == 0 else 0)) * TOK, TOK)]
            got = ps[:, 2 + u, 0:TOK * HALF].rearrange("p (t i) -> p i t", t=TOK)
            if half:
                v_.tensor_copy(dst, got).then_inc(g_read, 1)
            else:
                v_.tensor_tensor(dst, dst, got, ALU.mult).then_inc(g_read, 1)

        def meet(i, u):
            dve.wait_ge(gelu_ready, i + 1)
            v_.tensor_tensor(gated_tile(i), gated_tile(i), gelu[:, u, :], ALU.mult).then_inc(tile_ready, 1)

        plain(20, PLAIN_TILES)
        dve.wait_ge(ident_ready, 2)
        dve.wait_ge(slot_ready, 3)
        v_.tensor_tensor(gate_left[:], ps[:, 6, 0:SEQ], slot_gate[:, 0, :], ALU.subtract).then_inc(tail, 1)
        dve.wait_ge(tail, TAIL_OPS + 1)
        v_.tensor_copy(slot_gate[:, 1, :], gate_left[:]).then_inc(tail, 1)
        dve.wait_ge(tail, TAIL_OPS + 2)
        v_.tensor_tensor(slot_gate[:, 2, :], gate_left[:], slot_gate[:, 1, :], ALU.subtract).then_inc(tail, 1)
        dve.wait_ge(tail, TAIL_OPS + 3)
        for i in (PLAIN_TILES, PLAIN_TILES + 1):
            for v in range(2):
                s = 2 * (i - PLAIN_TILES) + v
                down_low(i // 2, i % 2, (2 * v, 2 * v + 1))
                onehots(s, v, 1, first=(s < 2))
                if s >= 2:
                    take(s - 2, v, 1)
        with dve.Fori(PLAIN_TILES // 2 + 1, HALF // 2) as it:
            for u in range(2):
                for v in range(2):
                    s = it * 4 + (2 * u + v - 2 * PLAIN_TILES)
                    down_low(it, u, (2 * v, 2 * v + 1))
                    onehots(s, v, 1)
                    take(s - 2, v, 1)
        for u in range(2):
            down_low(HALF // 2, u)
            onehots(STEPS + u, u, 0)
            take(STEPS - 2 + u, u, 1)
        dve.wait_ge(gelu_ready, HALF)
        dve.wait_ge(g_read, STEPS)
        meet(HALF, 0)
        with dve.Fori(HALF // 2 + 1, NKEYS // 2) as it:
            for u in range(2):
                down_low(it, u)
                onehots(it * 2 + u, u, 0)
                take(it * 2 + (u - 2), u, 0)
                meet(it * 2 + (u - 1), 1 - u)

        def low_gated(i, u):
            dve.wait_ge(ah_ready, i + 1)
            v_.tensor_tensor(al[:, u, :], gated_tile(i), ah[:, u, :].bitcast(F32), ALU.subtract).then_inc(al_ready, 1)

        q_up = Q_DOWN + 4 * NKEYS
        low(q_up, 8)
        for u in range(2):
            take(2 * STEPS - 2 + u, u, 0)
        meet(NKEYS - 1, 1)
        for u in range(2):
            low_gated(u, u)
        with dve.Fori(0, NKEYS // 2 - 1) as it:
            for u in range(2):
                low(q_up + 8 + 4 * u, 4, it)
                low_gated(it * 2 + (u + 2), u)

        dve.wait_ge(s_res2, 16)
        dve.wait_ge(s_fg, 16)
        dve.wait_ge(piece_used, Q_DOWN + 8 * NKEYS)
        for t in range(TT):
            for w in range(4):
                part = res2[:, t, w * 512:(w + 1) * 512]
                v_.tensor_tensor(part, part, ps[:, 4 * t + w, :], ALU.add).then_inc(h3_ready, 1)
        for t in range(TT):
            dve.wait_ge(ssq4, t + 1)
            v_.tensor_scalar(small[:, 6 + t:7 + t], small[:, 6 + t:7 + t], 1.0 / D, RMS_EPS, ALU.mult, ALU.add).then_inc(var4, 1)
            dve.wait_ge(std4, t + 1)
            v_.reciprocal(small[:, 6 + t:7 + t], small[:, 6 + t:7 + t]).then_inc(rs4, 1)
            dve.wait_ge(rs4, t + 1)
            v_.scalar_tensor_tensor(out=outb[:, t, :], in0=res2[:, t, :], scalar=small[:, 6 + t:7 + t], in1=fg[:],
                                    op0=ALU.mult, op1=ALU.mult).then_inc(fin, 1)

    ctx.close()


def kernel(**inputs):
    import numpy as np
    import concourse.bacc as bacc
    from concourse.bass_utils import run_bass_kernel_spmd

    a = {k: np.asarray(v) for k, v in inputs.items()}

    def columns(v, n):
        return v.reshape(n, P).T

    def stationary(w):
        rows, cols = w.shape
        w = w.reshape(rows // (8 * P), 8, P, cols // P, P).transpose(3, 0, 2, 1, 4)
        return w.reshape(-1, P, CHUNK)

    h = np.concatenate([a["meta_tokens"], a["x"][0]], axis=0)
    w_in = a["w_in"][0]
    conv = w_in[:, W:].reshape(D, 2, CT, P).transpose(0, 2, 1, 3).reshape(D, 2 * W)
    w_in = np.concatenate([conv, w_in[:, :W]], axis=1)
    pool_w = a["pool_w"][0].reshape(2, 2, 2, P, 2, P).transpose(0, 3, 1, 4, 2, 5).reshape(2, P, CHUNK)
    w_out = a["w_out"][0].reshape(2, CT, P, 2, CHUNK)[::-1].transpose(3, 0, 1, 2, 4).reshape(-1, P, CHUNK)
    front = np.concatenate([stationary(w_in), stationary(a["conv_pw_w"][0]), pool_w, w_out, stationary(a["peer_wq"][0])])
    assert front.shape[0] == FRONT
    dw = a["conv_dw_w"][0].reshape(TAPS, CT, P).transpose(2, 1, 0).reshape(P, CT * TAPS)
    vec = np.concatenate([
        columns(a["mix_norm_g"][0], KD), columns(a["pool_scale"][0], CT), dw, columns(a["conv_dw_b"][0], CT),
        columns(a["conv_ln_g"][0], CT), columns(a["conv_ln_b"][0], CT), columns(a["conv_pw_b"][0], CT),
        columns(a["ffn_norm_g"][0], KD)], axis=1)
    arrays = {
        "hT": h.T.reshape(KD, P, T).transpose(1, 0, 2),
        "x": a["x"][0].reshape(TT, P, D).transpose(1, 0, 2),
        "front": front,
        "down": a["peer_down"][0].reshape(NKEYS, P, 2, 8, P).transpose(0, 2, 4, 3, 1).reshape(2 * NKEYS, P, CHUNK),
        "up": a["peer_up"][0].reshape(NKEYS, P, 2, CHUNK).transpose(0, 2, 1, 3).reshape(2 * NKEYS, P, CHUNK),
        "keys": a["peer_keys"][0].transpose(3, 0, 1, 2).reshape(P, 2 * HEADS, NKEYS),
        "vec": vec,
        "fg": np.broadcast_to(a["final_norm_g"], (P, D)),
    }
    arrays = {f"in_{k}": np.ascontiguousarray(v) for k, v in arrays.items()}
    nc = bacc.Bacc("TRN2", target_bir_lowering=False, num_devices=1, dynamic_dma_scratch_size=1024)
    aps = [nc.dram_tensor(k, v.shape, mybir.dt.from_np(v.dtype), kind="ExternalInput").ap() for k, v in arrays.items()]
    out = nc.dram_tensor("out", (TT, P, D), F32, kind="ExternalOutput").ap()
    bass_hymba_peer_block(nc, *aps, out)
    r = run_bass_kernel_spmd(nc, [arrays], core_ids=[0])
    return r.results[0]["out"].reshape(1, SEQ, D)
```

```python
from contextlib import ExitStack

import concourse.bass as bass
from concourse import mybir

P = 128
F32 = mybir.dt.float32
F32R = mybir.dt.float32r
BF16 = mybir.dt.bfloat16
U32 = mybir.dt.uint32
ALU = mybir.AluOpType
ACT = mybir.ActivationFunctionType
AX = mybir.AxisListType

D = 2048
KD = D // P
META, SEQ = 16, 256
T = META + SEQ
TT = SEQ // P
W = 1024
CT = W // P
TAPS = 31
PAD = TAPS - 1 - META
WINDOWS = (2, 4, 8, 16)
HEADS, TOPK, NKEYS = 8, 16, 128
SLOTS = HEADS * TOPK
RMS_EPS, LN_EPS = 1e-6, 1e-5
LOWEST = -3.4028235e38

CHUNK = 1024
PROJ_TILES = 3 * CT
C_CONV = 4 * CT
C_PROJ = 2 * PROJ_TILES
C_PW = CT
C_POOL = 2
C_OUT = 2 * KD
C_WQ = 2 * KD
FRONT = C_PROJ + C_PW + C_POOL + C_OUT + C_WQ
RAW = 4
PIECE = CHUNK // 2
SPLIT = 8
Q_PW = 2 * (C_PROJ - C_CONV)
Q_POOL = Q_PW + 2 * C_PW
Q_OUT = Q_POOL + 2 * C_POOL
Q_WQ = Q_OUT + 2 * C_OUT
Q_DOWN = Q_WQ + 2 * C_WQ
PIECES_WQ = 2 * C_WQ
FIRST = 8
UP0 = FRONT + 2 * NKEYS
HALF = NKEYS // 2
TOK = 4
PARTS = 3
PLAIN_TILES = 32
ROUTE_TILE = 24
CONV_OPS = TAPS + 1
RANK_OPS = 32
RANK_READ = (6, 16)
TAIL_OPS = 19
STEPS = SEQ // TOK
WARM = 13

V_MIX, V_PS, V_DW, V_DB, V_LG, V_LB, V_PB, V_FFN = 0, 16, 24, 272, 280, 288, 296, 304
V_COLS = 320


def bass_hymba_peer_block(nc, hT_d, x_d, front_d, down_d, up_d, keys_d, vec_d, fg_d, out_d):
    spill_d = nc.dram_tensor("residual", (P, TT, D), F32, kind="Internal").ap()
    base = nc.sbuf_base + (-nc.sbuf_base) % 64
    top = [base]

    def at(name, shape, dt, offset):
        return nc.alloc_sbuf_tensor_at(name, shape, dt, offset=offset)

    def place(name, shape, dt):
        n = 2 if dt == BF16 else 4
        for s in shape[1:]:
            n *= s
        offset = top[0]
        top[0] += n + (-n) % 32
        return at(name, shape, dt, offset), offset

    gated, o_gated = place("gated", [P, NKEYS, SEQ], F32)
    raw, o_raw = place("raw", [P, RAW, CHUNK], F32)
    wh, _ = place("wh", [P, SPLIT, PIECE], F32R)
    wl, _ = place("wl", [P, SPLIT, PIECE], F32R)
    xh, o_xh = place("xh", [P, KD, SEQ], F32R)
    xl, o_xl = place("xl", [P, KD, SEQ], F32R)
    one_j, _ = place("one_j", [P, 2, P, TOK], BF16)
    one_i, o_one_i = place("one_i", [P, 2, HALF, TOK], BF16)
    gate_i, _ = place("gate_i", [P, 2, PARTS, HALF, TOK], BF16)
    gelu, o_gelu = place("gelu", [P, 2, SEQ], F32)
    slot_key, _ = place("slot_key", [P, 2, SEQ], BF16)
    slot_gate, _ = place("slot_gate", [P, PARTS, SEQ], BF16)
    small, _ = place("small", [P, 16], F32)
    ah, o_ah = place("ah", [P, 2, SEQ], F32R)
    al_0, _ = place("al_0", [P, SEQ], F32R)
    iota_tok, _ = place("iota_tok", [P, P, TOK], BF16)
    assert top[0] <= nc.sbuf_usable_end, (top[0], nc.sbuf_usable_end)
    al = [al_0, at("al_1", [P, SEQ], F32R, o_one_i)]
    ident = at("ident", [P, P], F32, o_ah)
    iota = at("iota", [P, P], F32, o_ah + 4 * P)
    hnh = at("hnh", [P, KD, T], F32R, o_xh)
    hnl = at("hnl", [P, KD, T], F32R, o_xh + 4 * KD * T)
    gate_left = at("gate_left", [P, SEQ], F32, o_gelu)

    def early(name, shape, offset, dt=F32):
        return at(name, shape, dt, o_gated + offset)

    hn = early("hn", [P, KD, T], 0)
    glu = early("glu", [P, CT, PAD + T], 17408)
    cv = early("cv", [P, CT, SEQ], 26624)
    xp = early("xp", [P, CT, T], 34816)
    sum_a = early("sum_a", [P, CT, T], 43520)
    sum_b = early("sum_b", [P, CT, T], 52224)
    squares = early("squares", [P, KD, T], 43520)
    hT = early("hT", [P, KD, T], 65536)
    sig = early("sig", [P, 2, T], 60928)
    odd = early("odd", [P, SEQ], 63232)
    pooled = early("pooled", [P, CT, SEQ], 65536)
    pooled_l = early("pooled_l", [P, CT, SEQ], 65536, F32R)
    cv_sq = early("cv_sq", [P, CT, SEQ], 73728)
    act_cv = early("act_cv", [P, CT, SEQ], 90112)
    act_l = early("act_l", [P, CT, SEQ], 90112, F32R)
    act_h = early("act_h", [P, CT, SEQ], 0, F32R)
    pooled_h = early("pooled_h", [P, CT, SEQ], 8192, F32R)
    res = early("res", [P, TT, D], 98304)
    rstd1 = early("rstd1", [P, T], 116864)
    rstd2 = early("rstd2", [P, SEQ], 118016)
    vec = early("vec", [P, V_COLS], 119040)
    ones = early("ones", [P, P], 120320)
    junk = early("junk", [P, D], 120832)
    xn = early("xn", [P, TT, D], 0)
    keys = early("keys", [P, 2 * HEADS, NKEYS], 65536)
    qT = early("qT", [P, 2, SEQ], 73728)
    sv = early("sv", [P, TT, HEADS, 2, TOPK], 75776)
    si_u = early("si_u", [P, TT, HEADS, 2, TOPK], 77824, U32)
    si = early("si", [P, TT, HEADS, 2, TOPK], 79872)
    left = early("left", [P, TT, NKEYS], 81920)
    cand = early("cand", [P, TT, TOPK * TOPK], 82944)
    cand_left = early("cand_left", [P, TT, TOPK * TOPK], 84992)
    topv = early("topv", [P, TT, HEADS, TOPK], 87040)
    pos = early("pos", [P, TT, HEADS, TOPK], 88064, U32)
    pos_u = early("pos_u", [P, 2, TT * SLOTS], 89088, U32)
    pos_f = early("pos_f", [P, 2, TT * SLOTS], 91136)
    route = early("route", [P, 3, TT, SLOTS], 93184)
    norm = early("norm", [P, 2, TT * HEADS], 96256)
    match = early("match", [P, SLOTS, TOPK], 120832)
    res2 = at("res2", [P, TT, D], F32, o_xl)
    fg = at("fg", [P, D], F32, o_xh)
    junk2 = at("junk2", [P, D], F32, o_xh + 8192)
    outb = at("outb", [P, TT, D], F32, o_raw)

    ctx = ExitStack()
    ps = ctx.enter_context(nc.psum_tensor("ps", [P, 8, 512], F32))

    def sem(name):
        return ctx.enter_context(nc.semaphore(name))

    s_hT = [sem(f"hT_loaded{g}") for g in range(4)]
    s_raw = [sem(f"raw_loaded{s}") for s in range(RAW)]
    s_vec, s_x, s_keys, s_fg, s_res2 = sem("vec_loaded"), sem("x_loaded"), sem("keys_loaded"), sem("fg_loaded"), sem("res2_loaded")
    s_spill, s_out = sem("residual_spilled"), sem("out_stored")
    ones_ready, iota_ready, pad_ready, ident_ready = sem("ones_ready"), sem("iota_ready"), sem("pad_ready"), sem("ident_ready")
    front_used, wh_ready, wl_ready, pool_low_ready, piece_used = (
        sem("front_used"), sem("wh_ready"), sem("wl_ready"), sem("pool_low_ready"), sem("piece_used"))
    hnh_ready, hnl_ready = sem("hnh_ready"), sem("hnl_ready")
    act_h_ready, act_l_ready, pooled_h_ready, pooled_l_ready = (
        sem("act_h_ready"), sem("act_l_ready"), sem("pooled_h_ready"), sem("pooled_l_ready"))
    warm, half_ssq, table_ready = sem("warm"), sem("half_ssq"), sem("table_ready")
    sq_ready, sq_added, ssq1, var1, std1, rs1, hn_ready = (
        sem("sq_ready"), sem("sq_added"), sem("ssq1"), sem("var1"), sem("std1"), sem("rs1"), sem("hn_ready"))
    gate_ready, value_ready, sig_ready, glu_ready, tap_done = (
        sem("gate_ready"), sem("value_ready"), sem("sig_ready"), sem("glu_ready"), sem("tap_done"))
    mean_done, xc_ready, cvsq_ready, var_done = sem("mean_done"), sem("xc_ready"), sem("cvsq_ready"), sem("var_done")
    var2, std2, rs2, ln_ready, silu_ready = sem("var2"), sem("std2"), sem("rs2"), sem("ln_ready"), sem("silu_ready")
    xp_ready, pool_step, pooled_ready = sem("xp_ready"), sem("pool_step"), sem("pooled_ready")
    yh_ready, yl_ready, res_ready = sem("yh_ready"), sem("yl_ready"), sem("res_ready")
    ssq3, sum3, var3, std3, rs3, xn_ready = sem("ssq3"), sem("sum3"), sem("var3"), sem("std3"), sem("rs3"), sem("xn_ready")
    xT_ps, xh_ready, xl_ready = sem("xT_ps"), sem("xh_ready"), sem("xl_ready")
    q_ready, score_done, rank = sem("q_ready"), sem("score_done"), sem("rank")
    z_ready, e_ready, tail, route_ps, slot_ready = sem("z_ready"), sem("e_ready"), sem("tail"), sem("route_ps"), sem("slot_ready")
    gelu_ready, tile_ready = sem("gelu_ready"), sem("tile_ready")
    eq_ready, onehot_ready, g_done, g_read = sem("eq_ready"), sem("onehot_ready"), sem("g_done"), sem("g_read")
    ah_ready, al_ready = sem("ah_ready"), sem("al_ready")
    quarter_done, h3_ready, ssq4, sum4 = sem("quarter_done"), sem("h3_ready"), sem("ssq4"), sem("sum4")
    var4, std4, rs4, fin = sem("var4"), sem("std4"), sem("rs4"), sem("fin")
    block = ctx.enter_context(nc.Block())

    def chunk(table, index):
        return table[bass.ds(index, 1)].rearrange("a p f -> (a p) f")

    def loads(c):
        return 16 * (c // RAW + 1)

    def gated_tile(i):
        return gated[:, bass.ds(i, 1), :].rearrange("p a t -> p (a t)")

    def bcast(ap, count):
        return ap.rearrange("p (n o) -> p n o", o=1).broadcast_to((P, ap.shape[1], count))

    def raw_piece(q):
        c = C_CONV + q // 2
        return raw[:, c % RAW, q % 2 * PIECE:(q % 2 + 1) * PIECE]

    def lows(q):
        return q - FIRST - (0 if q <= Q_WQ else PIECES_WQ)

    def low_piece(q):
        return wl[:, q % SPLIT, :], raw_piece(q), wh[:, q % SPLIT, :].bitcast(F32)

    @block.sync
    def _(sp):
        def load_tokens(g):
            sp.dma_start(hT[:, 4 * g:4 * g + 4, :], hT_d[:, 4 * g:4 * g + 4, :]).then_inc(s_hT[g], 16)

        load_tokens(0)
        sp.dma_start(vec[:], vec_d).then_inc(s_vec, 16)
        for c, groups in enumerate(((1, 2), (3,), (), ())):
            sp.dma_start(raw[:, c, :], chunk(front_d, c)).then_inc(s_raw[c], 16)
            for g in groups:
                load_tokens(g)
        def load_rows(part):
            cols = slice(part * 512, (part + 1) * 512)
            sp.dma_start(res[:, :, cols], x_d[:, :, cols]).then_inc(s_x, 16)

        load_rows(0)
        for part in range(4):
            lo = 1 + 2 * part
            with sp.Fori(lo, lo + 2) as it:
                for u in range(RAW):
                    sp.wait_ge(front_used, it * RAW + (u + 1 - RAW))
                    sp.dma_start(raw[:, u, :], chunk(front_d, it * RAW + u)).then_inc(s_raw[u], 16)
            if part < 3:
                load_rows(part + 1)

        def after_split(c, it=0):
            sp.wait_ge(wl_ready, it * (2 * RAW) + lows(2 * (c - RAW - C_CONV) + 2))

        for u in range(RAW):
            sp.wait_ge(pool_low_ready, 2 * u + 2)
            sp.dma_start(raw[:, u, :], chunk(front_d, C_CONV + RAW + u)).then_inc(s_raw[u], 16)
        first = C_CONV + 2 * RAW
        with sp.Fori(0, (FRONT - C_WQ - first) // RAW) as it:
            for u in range(RAW):
                after_split(first + u, it)
                sp.dma_start(raw[:, u, :], chunk(front_d, it * RAW + (first + u))).then_inc(s_raw[u], 16)
        sp.wait_ge(piece_used, Q_OUT)
        sp.dma_start(keys[:], keys_d).then_inc(s_keys, 16)
        for c in range(first + (FRONT - C_WQ - first) // RAW * RAW, FRONT - C_WQ + RAW):
            after_split(c)
            sp.dma_start(raw[:, c % RAW, :], chunk(front_d, c)).then_inc(s_raw[c % RAW], 16)
        with sp.Fori(1, C_WQ // RAW) as it:
            for u in range(RAW):
                c = FRONT - C_WQ + u
                sp.wait_ge(pool_low_ready, it * (2 * RAW) + (FIRST + 2 * (u - RAW) + 2))
                sp.dma_start(raw[:, c % RAW, :], chunk(front_d, it * RAW + c)).then_inc(s_raw[c % RAW], 16)
        for u in range(RAW):
            sp.wait_ge(pool_low_ready, FIRST + PIECES_WQ + 2 * (u - RAW) + 2)
            sp.dma_start(raw[:, (FRONT + u) % RAW, :], chunk(down_d, u)).then_inc(s_raw[(FRONT + u) % RAW], 16)
        for table, begin, skip in ((down_d, FRONT, 1), (up_d, UP0, 0)):
            with sp.Fori(skip, 2 * NKEYS // RAW) as it:
                for u in range(RAW):
                    after_split(begin + u + (RAW if skip else 0), it - 1 if skip else it)
                    slot = (begin + u) % RAW
                    sp.dma_start(raw[:, slot, :], chunk(table, it * RAW + u)).then_inc(s_raw[slot], 16)
        for t in range(TT):
            for w in range(4):
                sp.wait_ge(fin, 4 * t + w + 1)
                cols = slice(w * 512, (w + 1) * 512)
                sp.dma_start(out_d[t][:, cols], outb[:, t, cols]).then_inc(s_out, 16)
        sp.wait_ge(s_out, 16 * 4 * TT)

    @block.gpsimd
    def _(pool):
        nc.gpsimd.memset(ones[:], 1.0).then_inc(ones_ready, 1)
        nc.gpsimd.memset(glu[:, :, 0:PAD], 0.0).then_inc(pad_ready, 1)
        nc.gpsimd.iota(iota[:], [[1, P]], base=0, channel_multiplier=0,
                       allow_small_or_imprecise_dtypes=True).then_inc(iota_ready, 1)
        nc.gpsimd.iota(small[:, 0:1], [[0, 1]], base=0, channel_multiplier=1,
                       allow_small_or_imprecise_dtypes=True).then_inc(iota_ready, 1)
        for n, (a, b) in enumerate(((0, 4), (8, 12), (0, 8))):
            pool.wait_ge(*((sq_ready, 2 * n + 2) if n < 2 else (sq_added, 2)))
            nc.gpsimd.tensor_tensor(squares[:, a:a + 4, :], squares[:, a:a + 4, :], squares[:, b:b + 4, :],
                                    ALU.add).then_inc(sq_added, 1)
        for k in range(KD):
            pool.wait_ge(hnh_ready, k + 1)
            nc.gpsimd.tensor_tensor(hnl[:, k, :], hn[:, k, :], hnh[:, k, :].bitcast(F32), ALU.subtract).then_inc(hnl_ready, 1)
        for q in range(FIRST):
            pool.wait_ge(wh_ready, q + 1)
            nc.gpsimd.tensor_tensor(*low_piece(q), ALU.subtract).then_inc(pool_low_ready, 1)
        step = 0
        for g, window in enumerate(WINDOWS):
            tiles = slice(2 * g, 2 * g + 2)
            pool.wait_ge(xp_ready, 2 * g + 2)
            if g == 0:
                pool.wait_ge(rs1, 1)
                pool.wait_ge(ssq1, 1)
            nc.gpsimd.tensor_tensor(xp[:, tiles, :], xp[:, tiles, :],
                                    rstd1[:].rearrange("p (a t) -> p a t", a=1).broadcast_to((P, 2, T)),
                                    ALU.mult).then_inc(pool_step, 1)
            step += 1
            pool.wait_ge(pool_step, step)
            src, span = xp, 1
            while span < window:
                dst = sum_b if src is sum_a else sum_a
                lo = 2 * span - 1
                nc.gpsimd.tensor_tensor(dst[:, tiles, lo:T], src[:, tiles, lo:T], src[:, tiles, lo - span:T - span],
                                        ALU.add).then_inc(pool_step, 1)
                step += 1
                pool.wait_ge(pool_step, step)
                src, span = dst, 2 * span
            dst = sum_b if src is sum_a else sum_a
            nc.gpsimd.tensor_scalar(dst[:, tiles, META:T], src[:, tiles, META:T], 1.0 / window, None,
                                    ALU.mult).then_inc(pool_step, 1)
            step += 1
            pool.wait_ge(pool_step, step)
            nc.gpsimd.tensor_tensor(pooled[:, tiles, :], dst[:, tiles, META:T], xp[:, tiles, META:T],
                                    ALU.subtract).then_inc(pooled_ready, 1)
        with pool.Fori(0, 2 * HEADS // 2) as it:
            for u in range(2):
                for part in range(4):
                    q = Q_WQ + 4 * u + part
                    pool.wait_ge(wh_ready, it * 8 + (q + 1))
                    nc.gpsimd.tensor_tensor(*low_piece(q), ALU.subtract).then_inc(pool_low_ready, 1)

    @block.scalar
    def _(act):
        for g in range(4):
            act.wait_ge(s_hT[g], 16)
            nc.scalar.activation(squares[:, 4 * g:4 * g + 4, :], hT[:, 4 * g:4 * g + 4, :], ACT.Square).then_inc(sq_ready, 1)
        for k in range(KD):
            act.wait_ge(hn_ready, k + 1)
            nc.scalar.activation(hnh[:, k, :], hn[:, k, :], ACT.Copy).then_inc(hnh_ready, 1)

        act.wait_ge(var1, 1)
        nc.scalar.activation(rstd1[:], rstd1[:], ACT.Sqrt).then_inc(std1, 1)

        def glu_gate(c, u):
            act.wait_ge(gate_ready, c + 1)
            nc.scalar.activation(sig[:, u, :], sig[:, u, :], ACT.Sigmoid).then_inc(sig_ready, 1)

        def high(q, count, it=0):
            for n in range(q, q + count):
                c = C_CONV + n // 2
                if n % 2 == 0:
                    act.wait_ge(s_raw[c % RAW], it * 16 + loads(c))
                if n >= SPLIT:
                    act.wait_ge(piece_used, it * 8 + (n - SPLIT + 1))
                nc.scalar.activation(wh[:, n % SPLIT, :], raw_piece(n), ACT.Copy).then_inc(wh_ready, 1)

        for u in range(2):
            glu_gate(u, u)
        with act.Fori(1, CT // 2 - 1) as it:
            for u in range(2):
                glu_gate(it * 2 + u, u)
        for u in range(2):
            glu_gate(CT - 2 + u, u)
            high(6 * u, 6 - 4 * u)

        def keep_xp(n):
            act.wait_ge(piece_used, 4 * (n + 1))
            nc.scalar.activation(xp[:, n, :], ps[:, n % 4, 0:T], ACT.Copy).then_inc(xp_ready, 1)

        def pool_columns(n):
            high(4 * (n + 2), 3)
            keep_xp(n)
            high(4 * (n + 2) + 3, 1)

        for n in range(2):
            pool_columns(n)
        act.wait_ge(xc_ready, 1)
        nc.scalar.activation(cv_sq[:], cv[:], ACT.Square).then_inc(cvsq_ready, 1)
        for n in range(2, 5):
            pool_columns(n)
        act.wait_ge(var2, 1)
        nc.scalar.activation(rstd2[:], rstd2[:], ACT.Sqrt).then_inc(std2, 1)
        pool_columns(5)
        act.wait_ge(ln_ready, 1)
        for k in range(CT):
            nc.scalar.activation(act_cv[:, k, :], cv[:, k, :], ACT.Silu, bias=vec[:, V_LB + k:V_LB + k + 1],
                                 scale=vec[:, V_LG + k:V_LG + k + 1]).then_inc(silu_ready, 1)
        keep_xp(6)
        act.wait_ge(silu_ready, CT)
        for k in range(CT):
            nc.scalar.activation(act_h[:, k, :], act_cv[:, k, :], ACT.Copy).then_inc(act_h_ready, 1)
        high(Q_PW, 4)
        keep_xp(7)
        high(Q_PW + 4, 4)

        for m in range(CT):
            act.wait_ge(piece_used, Q_PW + 2 * m + 2)
            nc.scalar.activation(xh[:, CT + m, :], ps[:, m % 4, 0:SEQ], ACT.Identity,
                                 bias=vec[:, V_PB + m:V_PB + m + 1]).then_inc(yh_ready, 1)
            high(Q_PW + 8 + 2 * m, 2)
            if m % 2:
                g = m // 2
                act.wait_ge(pooled_ready, g + 1)
                nc.scalar.activation(pooled_h[:, 2 * g:2 * g + 2, :], pooled[:, 2 * g:2 * g + 2, :],
                                     ACT.Copy).then_inc(pooled_h_ready, 1)
        for m in range(CT):
            act.wait_ge(piece_used, Q_POOL + m // 2 + 1)
            nc.scalar.activation(xh[:, m, :], ps[:, m % 4, 0:SEQ], ACT.Copy,
                                 scale=vec[:, V_PS + m:V_PS + m + 1]).then_inc(yh_ready, 1)
        high(Q_OUT + 4, 4)
        with act.Fori(1, 5) as it:
            high(Q_OUT, 8, it)
        for t in range(TT):
            act.wait_ge(res_ready, 2 * t + 2)
            nc.scalar.activation(junk[:, t * 1024:(t + 1) * 1024], res[:, t, 0:1024], ACT.Square,
                                 accum_out=small[:, 8 + 3 * t:9 + 3 * t]).then_inc(half_ssq, 1)
        with act.Fori(5, 2 * C_OUT // 8) as it:
            high(Q_OUT, 8, it)
        high(Q_WQ, 6)
        act.wait_ge(half_ssq, TT)
        nc.scalar.activation(small[:, 1:2], small[:, 0:1], ACT.Sqrt).then_inc(table_ready, 1)
        for w in range(2):
            for t in range(TT):
                n = 2 * w + t
                act.wait_ge(res_ready, 4 + n + 1)
                nc.scalar.activation(junk[:, n * 512:(n + 1) * 512], res[:, t, 1024 + w * 512:1536 + w * 512], ACT.Square,
                                     accum_out=small[:, 9 + 3 * t + w:10 + 3 * t + w]).then_inc(ssq3, 1)
        act.wait_ge(var3, 1)
        nc.scalar.activation(small[:, 2:4], small[:, 2:4], ACT.Sqrt).then_inc(std3, 1)
        high(Q_WQ + 6, 2)
        act.dma_start(spill_d, res[:]).then_inc(s_spill, 16)
        for k in range(KD):
            act.wait_ge(xT_ps, k + 1)
            nc.scalar.activation(xh[:, k, :], ps[:, 2 + k % 6, 0:SEQ], ACT.Copy,
                                 scale=vec[:, V_FFN + k:V_FFN + k + 1]).then_inc(xh_ready, 1)

        def query(n, u):
            act.wait_ge(piece_used, n * 4 + (Q_WQ + 4))
            nc.scalar.activation(qT[:, u, :], ps[:, u, 0:SEQ], ACT.Copy).then_inc(q_ready, 1)

        for u in range(2):
            query(u, u)
            high(Q_WQ + 8 + 4 * u, 4)
        with act.Fori(1, HEADS) as it:
            for u in range(2):
                act.wait_ge(score_done, it * 2 + (u - 1))
                query(it * 2 + u, u)
                high(Q_WQ + 8 + 4 * u, 4, it)

        def gelu_into(out, i, u):
            act.wait_ge(piece_used, i * 4 + (Q_DOWN + 4))
            nc.scalar.activation(out, ps[:, u, 0:SEQ], ACT.Gelu).then_inc(gelu_ready, 1)

        act.wait_ge(s_spill, 16)

        def direct_tiles(lo, hi):
            with act.Fori(lo // 2, hi // 2) as it:
                for u in range(2):
                    gelu_into(gated_tile(it * 2 + u), it * 2 + u, u)
                    high(Q_DOWN + 8 + 4 * u, 4, it)

        for u in range(2):
            gelu_into(gated_tile(u), u, u)
            high(Q_DOWN + 8 + 4 * u, 4)
        act.wait_ge(z_ready, 1)
        nc.scalar.activation(route[:, 2], route[:, 2], ACT.Exp).then_inc(e_ready, 1)
        direct_tiles(2, ROUTE_TILE)
        act.wait_ge(route_ps, 1)
        for r in range(2):
            nc.scalar.activation(slot_key[:, r, :], ps[:, 4 + r, 0:SEQ], ACT.Copy).then_inc(slot_ready, 1)
        nc.scalar.activation(slot_gate[:, 0, :], ps[:, 6, 0:SEQ], ACT.Copy).then_inc(slot_ready, 1)
        direct_tiles(ROUTE_TILE, HALF)
        for i in (HALF, HALF + 1):
            gelu_into(gelu[:, i % 2, :], i, i % 2)
            high(Q_DOWN + 8 + 4 * (i % 2), 4, HALF // 2)
        def high_gated(i, u):
            nc.scalar.activation(ah[:, u, :], gated_tile(i), ACT.Copy).then_inc(ah_ready, 1)

        with act.Fori(HALF // 2 + 1, NKEYS // 2 - 1) as it:
            for u in range(2):
                act.wait_ge(tile_ready, it * 2 + (u - HALF - 1))
                gelu_into(gelu[:, u, :], it * 2 + u, u)
                high(Q_DOWN + 8 + 4 * u, 4, it)
        for u in range(2):
            i = NKEYS - 2 + u
            act.wait_ge(tile_ready, i - HALF - 1)
            gelu_into(gelu[:, u, :], i, u)
            high(Q_DOWN + 4 * i + 8, 4)
            if u == 0:
                for n in range(2):
                    high_gated(HALF + n, n)

        act.wait_ge(tile_ready, NKEYS - HALF)
        act.wait_ge(g_read, 2 * STEPS)
        q_up = Q_DOWN + 4 * NKEYS
        for lo, hi, shift in ((0, HALF // 2 - 1, HALF), (HALF // 2 - 1, NKEYS // 2 - 1, -HALF)):
            with act.Fori(lo, hi) as it:
                for u in range(2):
                    high(q_up + 8 + 4 * u, 4, it)
                    high_gated(it * 2 + (u + 2 + shift), u)
            if shift > 0:
                act.dma_start(res2[:], spill_d).then_inc(s_res2, 16)
                act.dma_start(fg[:], fg_d).then_inc(s_fg, 16)
        nc.scalar.activation(small[:, 1:2], small[:, 0:1], ACT.Sqrt).then_inc(table_ready, 1)
        for t in range(TT):
            for w in range(4):
                act.wait_ge(h3_ready, 4 * t + w + 1)
                if t:
                    act.wait_ge(ssq4, w + 1)
                nc.scalar.activation(junk2[:, w * 512:(w + 1) * 512],
                                     res2[:, t, w * 512:(w + 1) * 512], ACT.Square,
                                     accum_out=small[:, 8 + 4 * t + w:9 + 4 * t + w]).then_inc(ssq4, 1)
            act.wait_ge(var4, t + 1)
            nc.scalar.activation(small[:, 6 + t:7 + t], small[:, 6 + t:7 + t], ACT.Sqrt).then_inc(std4, 1)

    @block.tensor
    def _(pe):
        matmul = nc.tensor.matmul
        pe.wait_ge(ones_ready, 1)
        for _ in range(WARM):
            m = matmul(ps[:, 7, 0:P], ones[:], ones[:], start=True, stop=True)
        m.then_inc(warm, 1)

        def proj_tile(it, u, first=False):
            for half in range(2):
                c = 2 * u + half
                pe.wait_ge(s_raw[c % RAW], it * 32 + loads(c))
                for k in range(8):
                    kk = 8 * half + k
                    if first:
                        pe.wait_ge(hn_ready, kk + 1)
                    m = matmul(ps[:, u, 0:T], raw[:, c % RAW, k * P:(k + 1) * P], hn[:, kk, :],
                               start=(kk == 0), stop=(kk == KD - 1))
                m.then_inc(front_used, 1)

        for u in range(4):
            proj_tile(0, u, first=(u == 0))
            if u == 1:
                pe.wait_ge(sq_added, 3)
                for k in range(4):
                    m = matmul(ps[:, 4, 0:T], ones[:], squares[:, k, :], start=(k == 0), stop=(k == 3))
                m.then_inc(ssq1, 1)
        with pe.Fori(1, 2 * CT // 4) as it:
            for u in range(4):
                if u % 2 == 0:
                    pe.wait_ge(glu_ready, it * 2 + (u // 2 - 1))
                proj_tile(it, u)

        def split_products(out, weights, high_x, low_x, start, stop, swap=False):
            slot, cols = weights
            w_h, w_l = wh[:, slot, cols], wl[:, slot, cols]
            for a, b, begin, end in ((w_h, high_x, start, False), (w_h, low_x, False, False), (w_l, high_x, False, stop)):
                m = matmul(out, b, a, start=begin, stop=end) if swap else matmul(out, a, b, start=begin, stop=end)
            return m

        def piece_ready(q, it=0):
            if q < FIRST:
                pe.wait_ge(pool_low_ready, q + 1)
            elif Q_WQ <= q < Q_DOWN:
                pe.wait_ge(pool_low_ready, it * 8 + (FIRST + q - Q_WQ + 1))
            else:
                pe.wait_ge(wl_ready, it * 8 + lows(q + 1))

        def block_cols(k):
            return slice(k * P, (k + 1) * P)

        def pool_tile(n):
            if n < 4:
                pe.wait_ge(glu_ready, CT - 1 + n // 2)
            else:
                pe.wait_ge(xp_ready, n - 3)
            for part in range(4):
                q = 4 * n + part
                piece_ready(q)
                for k in range(4):
                    kk = 4 * part + k
                    if n == 0:
                        pe.wait_ge(hnl_ready, kk + 1)
                    m = split_products(ps[:, n % 4, 0:T], (q % SPLIT, block_cols(k)), hnh[:, kk, :], hnl[:, kk, :],
                                       kk == 0, kk == KD - 1)
                m.then_inc(piece_used, 1)

        for n in range(3):
            pool_tile(n)
        for k in range(CT):
            pe.wait_ge(tap_done, CONV_OPS * (k + 1))
            m = matmul(ps[:, 5, 0:SEQ], ones[:], cv[:, k, :], start=(k == 0), stop=(k == CT - 1))
        m.then_inc(mean_done, 1)
        for n in range(3, 5):
            pool_tile(n)
        pe.wait_ge(cvsq_ready, 1)
        for k in range(CT):
            m = matmul(ps[:, 6, 0:SEQ], ones[:], cv_sq[:, k, :], start=(k == 0), stop=(k == CT - 1))
        m.then_inc(var_done, 1)
        for n in range(5, 8):
            pool_tile(n)

        for m in range(CT):
            if m < 4:
                pe.wait_ge(xp_ready, 5 + m)
            else:
                pe.wait_ge(yl_ready, m - 3)
            for part in range(2):
                q = Q_PW + 2 * m + part
                piece_ready(q)
                for k in range(4):
                    kk = 4 * part + k
                    if m == 0:
                        pe.wait_ge(act_l_ready, kk + 1)
                    last = split_products(ps[:, m % 4, 0:SEQ], (q % SPLIT, block_cols(k)), act_h[:, kk, :],
                                          act_l[:, kk, :], kk == 0, kk == CT - 1)
                last.then_inc(piece_used, 1)
        for g in range(len(WINDOWS)):
            q = Q_POOL + g
            piece_ready(q)
            pe.wait_ge(pooled_l_ready, g + 1)
            for d in range(2):
                m = 2 * g + d
                pe.wait_ge(yl_ready, CT + m - 3)
                for k in range(2):
                    last = split_products(ps[:, m % 4, 0:SEQ], (q % SPLIT, block_cols(2 * d + k)),
                                          pooled_h[:, 2 * g + k, :], pooled_l[:, 2 * g + k, :], k == 0, k == 1)
            last.then_inc(piece_used, 1)

        for half in range(2):
            for n in range(KD):
                k = (n + CT) % KD
                pe.wait_ge(yl_ready, n + 1 if half == 0 else KD)
                for w in range(2):
                    q = Q_OUT + 2 * (half * KD + n) + w
                    piece_ready(q)
                    for t in range(TT):
                        tok = slice(t * P, (t + 1) * P)
                        last = split_products(ps[:, 4 * (1 - half) + 2 * t + w, :], (q % SPLIT, slice(0, PIECE)),
                                              xh[:, k, tok], xl[:, k, tok], n == 0, n == KD - 1, swap=True)
                    last.then_inc(piece_used, 1)

        def query(it, v, first=False):
            if not first:
                pe.wait_ge(q_ready, it * 4 + (v - 1))
            for part in range(4):
                q = Q_WQ + 4 * v + part
                piece_ready(q, it * 2)
                for k in range(4):
                    kk = 4 * part + k
                    m = split_products(ps[:, v % 2, 0:SEQ], (q % SPLIT, block_cols(k)), xh[:, kk, :], xl[:, kk, :],
                                       kk == 0, kk == KD - 1)
                m.then_inc(piece_used, 1)

        def scores(it, v, first=False):
            head, half = v // 2, v % 2
            pe.wait_ge(q_ready, it * 4 + (v + 1))
            if not first:
                pe.wait_ge(rank, it * (2 * RANK_OPS) + ((head - 2) * RANK_OPS + RANK_READ[half]))
            for t in range(TT):
                key = keys[:, bass.ds(it * 4 + v, 1), :].rearrange("p a n -> p (a n)")
                m = matmul(ps[:, 2 + v, t * P:(t + 1) * P], qT[:, half, t * P:(t + 1) * P], key, start=True, stop=True)
            m.then_inc(score_done, 1)

        pe.wait_ge(ident_ready, 1)
        for k in range(KD + 6):
            if k < KD:
                if k >= 6:
                    pe.wait_ge(xl_ready, k - 5)
                for t in range(TT):
                    pe.wait_ge(xn_ready, k // 4 * TT + t + 1)
                    last = nc.tensor.transpose(ps[:, 2 + k % 6, t * P:(t + 1) * P], xn[:, t, k * P:(k + 1) * P], ident[:])
                last.then_inc(xT_ps, 1)
            kk = k - 6
            if kk >= 0:
                q = Q_WQ + kk // 4
                piece_ready(q)
                pe.wait_ge(xl_ready, kk + 1)
                last = split_products(ps[:, 0, 0:SEQ], (q % SPLIT, block_cols(kk % 4)), xh[:, kk, :], xl[:, kk, :],
                                      kk == 0, kk == KD - 1)
                if kk % 4 == 3:
                    last.then_inc(piece_used, 1)
        pe.wait_ge(s_keys, 16)
        for v in range(1, 4):
            query(0, v, first=(v == 1))
            scores(0, v - 1, first=True)

        def queries(it, first=False):
            query(it, 0)
            scores(it - 1, 3, first=first)
            for v in range(1, 4):
                query(it, v)
                scores(it, v - 1)

        queries(1, first=True)
        with pe.Fori(2, HEADS // 2) as it:
            queries(it)
        scores(HEADS // 2 - 1, 3)

        def down_tile(it, u, first=False, steps=()):
            if not first:
                pe.wait_ge(gelu_ready, it * 2 + (u - 1))
            for part in range(4):
                q = Q_DOWN + 4 * u + part
                piece_ready(q, it)
                for k in range(4):
                    kk = 4 * part + k
                    m = split_products(ps[:, u, 0:SEQ], (q % SPLIT, block_cols(k)), xh[:, kk, :], xl[:, kk, :],
                                       kk == 0, kk == KD - 1)
                m.then_inc(piece_used, 1)
                if part % 2 and part // 2 < len(steps):
                    gate_step(*steps[part // 2])

        def gate_step(s, slot, first=False):
            if not first:
                pe.wait_ge(g_read, s - 1)
            pe.wait_ge(onehot_ready, s + 1)
            for n, part in [(n, part) for n in range(TOK) for part in range(PARTS)]:
                m = matmul(ps[:, 2 + slot, n * HALF:(n + 1) * HALF], one_j[:, slot, :, n],
                           gate_i[:, slot, part, :, n], start=(part == 0), stop=(part == PARTS - 1))
            m.then_inc(g_done, 1)

        for u in range(2):
            pe.wait_ge(q_ready, 2 * HEADS - 1 + u)
            down_tile(0, u, first=True)
        with pe.Fori(1, ROUTE_TILE // 2) as it:
            for u in range(2):
                down_tile(it, u)
        pe.wait_ge(tail, TAIL_OPS)
        for r in range(3):
            for t in range(TT):
                m = nc.tensor.transpose(ps[:, 4 + r, t * P:(t + 1) * P], route[:, r, t, :], ident[:])
        m.then_inc(route_ps, 1)
        with pe.Fori(ROUTE_TILE // 2, PLAIN_TILES // 2) as it:
            for u in range(2):
                down_tile(it, u)
        down_tile(PLAIN_TILES // 2, 0, steps=((0, 0, True), (1, 1, True)))
        down_tile(PLAIN_TILES // 2, 1, steps=((2, 0), (3, 1)))
        with pe.Fori(PLAIN_TILES // 2 + 1, HALF // 2) as it:
            for u in range(2):
                down_tile(it, u, steps=[(it * 4 + (2 * u + v - 2 * PLAIN_TILES), v) for v in range(2)])
        with pe.Fori(HALF // 2, NKEYS // 2) as it:
            for u in range(2):
                down_tile(it, u, steps=[(it * 2 + u, u)])

        q_up = Q_DOWN + 4 * NKEYS

        def up_part(t, u, part, start=False, stop=False):
            tok = slice(t * P, (t + 1) * P)
            return split_products(ps[:, 4 * t + part, :], ((q_up + 4 * u + part) % SPLIT, slice(0, PIECE)), ah[:, u, tok],
                                  al[u][:, tok], start, stop, swap=True)

        def up_tile(it, u, start=False):
            pe.wait_ge(al_ready, it * 2 + (u + 1))
            for part in range(4):
                piece_ready(q_up + 4 * u + part, it)
                if start:
                    pe.wait_ge(*((gelu_ready, NKEYS - 1 + part) if part < 2 else (g_read, 2 * STEPS)))
                for t in range(TT):
                    m = up_part(t, u, part, start)
                m.then_inc(piece_used, 1)

        up_tile(0, 0, start=True)
        up_tile(0, 1)
        with pe.Fori(1, NKEYS // 2 - 1) as it:
            for u in range(2):
                up_tile(it, u)
        for t in range(TT):
            for u in range(2):
                pe.wait_ge(al_ready, NKEYS - 1 + u)
                for part in range(4):
                    piece_ready(Q_DOWN + 4 * (2 * NKEYS - 2 + u) + part)
                    m = up_part(t, u, part, stop=(u == 1))
                    if u == 1:
                        m.then_inc(quarter_done, 1)

    @block.vector
    def _(dve):
        v_ = nc.vector
        dve.wait_ge(iota_ready, 2)
        v_.tensor_scalar(ident[:], iota[:], small[:, 0:1], None, ALU.is_equal).then_inc(ident_ready, 1)
        v_.tensor_copy(iota_tok[:], bcast(iota[:], TOK)).then_inc(ident_ready, 1)
        dve.wait_ge(s_vec, 16)
        for k in range(KD):
            if k % 4 == 0:
                dve.wait_ge(s_hT[k // 4], 16)
            v_.tensor_scalar(hn[:, k, :], hT[:, k, :], vec[:, V_MIX + k:V_MIX + k + 1], None, ALU.mult).then_inc(hn_ready, 1)
        dve.wait_ge(ssq1, 1)
        v_.tensor_scalar(rstd1[:], ps[:, 4, 0:T], 1.0 / D, RMS_EPS, ALU.mult, ALU.add).then_inc(var1, 1)
        dve.wait_ge(std1, 1)
        v_.reciprocal(rstd1[:], rstd1[:]).then_inc(rs1, 1)
        dve.wait_ge(rs1, 1)

        def low(q, count=4, it=0):
            for n in range(q, q + count):
                dve.wait_ge(wh_ready, it * 8 + (n + 1))
                v_.tensor_tensor(*low_piece(n), ALU.subtract).then_inc(wl_ready, 1)

        def conv_tile(c, u, pieces=()):
            dve.wait_ge(front_used, c * 4 + 4)
            v_.tensor_tensor(sig[:, u, :], ps[:, 2 * u + 1, 0:T], rstd1[:], ALU.mult).then_inc(gate_ready, 1)
            value = glu[:, bass.ds(c, 1), PAD:PAD + T].rearrange("p a t -> p (a t)")
            v_.tensor_tensor(value, ps[:, 2 * u, 0:T], rstd1[:], ALU.mult).then_inc(value_ready, 1)
            dve.wait_ge(value_ready, c + 1)
            dve.wait_ge(sig_ready, c + 1)
            v_.tensor_tensor(value, value, sig[:, u, :], ALU.mult).then_inc(glu_ready, 1)
            dve.wait_ge(glu_ready, c + 1)
            acc = cv[:, bass.ds(c, 1), :].rearrange("p a t -> p (a t)")
            for j in range(TAPS):
                x = glu[:, bass.ds(c, 1), j:j + SEQ].rearrange("p a t -> p (a t)")
                w = vec[:, bass.ds(c * TAPS + (V_DW + j), 1)]
                if j in pieces:
                    low(*pieces[j])
                if j >= 2:
                    dve.wait_ge(tap_done, c * CONV_OPS + (j - 1))
                if j == 0:
                    ins = v_.tensor_scalar(acc, x, w, vec[:, bass.ds(c + V_DB, 1)], ALU.mult, ALU.add)
                elif j == 1:
                    ins = v_.tensor_scalar(odd[:], x, w, None, ALU.mult)
                else:
                    dst = odd[:] if j % 2 else acc
                    ins = v_.scalar_tensor_tensor(out=dst, in0=x, scalar=w, in1=dst, op0=ALU.mult, op1=ALU.add)
                ins.then_inc(tap_done, 1)
            dve.wait_ge(tap_done, c * CONV_OPS + TAPS)
            v_.tensor_tensor(acc, acc, odd[:], ALU.add).then_inc(tap_done, 1)
            dve.wait_ge(tap_done, c * CONV_OPS + CONV_OPS)

        dve.wait_ge(pad_ready, 1)
        with dve.Fori(0, CT // 2 - 1) as it:
            for u in range(2):
                conv_tile(it * 2 + u, u)
        conv_tile(CT - 2, 0)
        conv_tile(CT - 1, 1, pieces={10: (8, 2), 18: (10, 2)})
        low(12, 4)
        dve.wait_ge(mean_done, 1)
        mean = ps[:, 5:6, 0:SEQ].broadcast_to((P, CT, SEQ))
        v_.scalar_tensor_tensor(out=cv[:], in0=mean, scalar=-1.0 / W, in1=cv[:], op0=ALU.mult, op1=ALU.add).then_inc(xc_ready, 1)
        low(16, 8)
        dve.wait_ge(var_done, 1)
        v_.tensor_scalar(rstd2[:], ps[:, 6, 0:SEQ], 1.0 / W, LN_EPS, ALU.mult, ALU.add).then_inc(var2, 1)
        low(24, 4)
        dve.wait_ge(std2, 1)
        v_.reciprocal(rstd2[:], rstd2[:]).then_inc(rs2, 1)
        dve.wait_ge(rs2, 1)
        v_.tensor_tensor(cv[:], cv[:], rstd2[:].rearrange("p (a t) -> p a t", a=1).broadcast_to((P, CT, SEQ)),
                         ALU.mult).then_inc(ln_ready, 1)
        low(28, 4)
        for k in range(CT):
            dve.wait_ge(act_h_ready, k + 1)
            v_.tensor_tensor(act_l[:, k, :], act_cv[:, k, :], act_h[:, k, :].bitcast(F32), ALU.subtract).then_inc(act_l_ready, 1)
        low(Q_PW, 8)
        for m in range(CT):
            dve.wait_ge(yh_ready, m + 1)
            v_.scalar_tensor_tensor(out=xl[:, CT + m, :], in0=ps[:, m % 4, 0:SEQ], scalar=vec[:, V_PB + m:V_PB + m + 1],
                                    in1=xh[:, CT + m, :].bitcast(F32), op0=ALU.add, op1=ALU.subtract).then_inc(yl_ready, 1)
            low(Q_PW + 8 + 2 * m, 2)
            if m % 2:
                g = m // 2
                dve.wait_ge(pooled_h_ready, g + 1)
                v_.tensor_tensor(pooled_l[:, 2 * g:2 * g + 2, :], pooled[:, 2 * g:2 * g + 2, :],
                                 pooled_h[:, 2 * g:2 * g + 2, :].bitcast(F32), ALU.subtract).then_inc(pooled_l_ready, 1)
        for m in range(CT):
            dve.wait_ge(yh_ready, CT + m + 1)
            v_.scalar_tensor_tensor(out=xl[:, m, :], in0=ps[:, m % 4, 0:SEQ], scalar=vec[:, V_PS + m:V_PS + m + 1],
                                    in1=xh[:, m, :].bitcast(F32), op0=ALU.mult, op1=ALU.subtract).then_inc(yl_ready, 1)
        low(Q_OUT + 4, 4)
        with dve.Fori(1, 5) as it:
            low(Q_OUT, 8, it)
        dve.wait_ge(s_x, 16 * 4)

        def join(half, w, t):
            part = res[:, t, half * 1024 + w * 512:half * 1024 + w * 512 + 512]
            v_.tensor_tensor(part, part, ps[:, 4 * (1 - half) + 2 * t + w, :], ALU.add).then_inc(res_ready, 1)

        dve.wait_ge(piece_used, Q_OUT + 2 * KD)
        for t in range(TT):
            for w in range(2):
                join(0, w, t)
        with dve.Fori(5, 2 * C_OUT // 8) as it:
            low(Q_OUT, 8, it)
        for w in range(2):
            dve.wait_ge(piece_used, Q_WQ - 1 + w)
            for t in range(TT):
                join(1, w, t)
        dve.wait_ge(ssq3, 2 * TT)
        dve.wait_ge(half_ssq, TT)
        v_.tensor_reduce(small[:, 2:4], small[:, 8:14].rearrange("p (t n) -> p t n", t=TT), AX.X, ALU.add).then_inc(sum3, 1)
        dve.wait_ge(sum3, 1)
        v_.tensor_scalar(small[:, 2:4], small[:, 2:4], 1.0 / D, RMS_EPS, ALU.mult, ALU.add).then_inc(var3, 1)
        dve.wait_ge(std3, 1)
        v_.reciprocal(small[:, 2:4], small[:, 2:4]).then_inc(rs3, 1)
        dve.wait_ge(rs3, 1)
        for w in range(4):
            for t in range(TT):
                v_.tensor_scalar(xn[:, t, w * 512:(w + 1) * 512], res[:, t, w * 512:(w + 1) * 512], small[:, 2 + t:3 + t], None,
                                 ALU.mult).then_inc(xn_ready, 1)

        for k in range(KD):
            dve.wait_ge(xh_ready, k + 1)
            v_.scalar_tensor_tensor(out=xl[:, k, :], in0=ps[:, 2 + k % 6, 0:SEQ], scalar=vec[:, V_FFN + k:V_FFN + k + 1],
                                    in1=xh[:, k, :].bitcast(F32), op0=ALU.mult, op1=ALU.subtract).then_inc(xl_ready, 1)

        done = [0]

        def ranked(ins):
            ins.then_inc(rank, 1)
            done[0] += 1
            if done[0] >= 2:
                dve.wait_ge(rank, done[0] - 1)

        def top16(values, indices, source, rest):
            for t in range(TT):
                ranked(v_.max(values(t)[:, 0:8], source(t)))
            for t in range(TT):
                ranked(v_.max_index(indices(t)[:, 0:8], values(t)[:, 0:8], source(t)))
            for t in range(TT):
                ranked(v_.match_replace(rest(t), values(t)[:, 0:8], source(t), LOWEST))
            for t in range(TT):
                ranked(v_.max(values(t)[:, 8:16], rest(t)))
            for t in range(TT):
                ranked(v_.max_index(indices(t)[:, 8:16], values(t)[:, 8:16], rest(t)))

        for h in range(HEADS):
            for half in range(2):
                if h == HEADS - 1:
                    low(Q_DOWN + 4 * half, 4)
                dve.wait_ge(score_done, 2 * h + half + 1)
                top16(lambda t: sv[:, t, h, half, :], lambda t: si_u[:, t, h, half, :],
                      lambda t: ps[:, 2 + h % 2 * 2 + half, t * P:(t + 1) * P], lambda t: left[:, t, :])
            for t in range(TT):
                first = bcast(sv[:, t, h, 0, :], TOPK)
                second = sv[:, t, h, 1:2, :].broadcast_to((P, TOPK, TOPK))
                ranked(v_.tensor_tensor(cand[:, t, :].rearrange("p (a b) -> p a b", a=TOPK), first, second, ALU.add))
            if h == HEADS - 1:
                low(Q_DOWN + 8, 4)
            top16(lambda t: topv[:, t, h, :], lambda t: pos[:, t, h, :], lambda t: cand[:, t, :], lambda t: cand_left[:, t, :])
            assert done[0] == RANK_OPS * (h + 1)
        dve.wait_ge(rank, RANK_OPS * HEADS)

        def down_low(it, u, parts=range(4)):
            for part in parts:
                low(Q_DOWN + 4 * u + part, 1, it)

        steps = [0]

        def tailed(ins):
            ins.then_inc(tail, 1)
            steps[0] += 1

        flat = "p t h k -> p (t h k)"
        top = topv[:].rearrange("p t h k -> p (t h) k")
        exp_ = route[:, 2].rearrange("p t (h k) -> p (t h) k", h=HEADS)
        down_low(1, 1)
        v_.tensor_tensor(exp_, top, top[:, :, 0:1].broadcast_to((P, TT * HEADS, TOPK)), ALU.subtract).then_inc(z_ready, 1)
        tailed(v_.tensor_copy(si[:].rearrange("p t h c k -> p (t h c k)"), si_u[:].rearrange("p t h c k -> p (t h c k)")))
        tailed(v_.tensor_scalar(pos_u[:, 0, :], pos[:].rearrange(flat), 4, None, ALU.logical_shift_right))
        tailed(v_.tensor_scalar(pos_u[:, 1, :], pos[:].rearrange(flat), TOPK - 1, None, ALU.bitwise_and))
        dve.wait_ge(tail, 3)
        tailed(v_.tensor_copy(pos_f[:], pos_u[:]))
        dve.wait_ge(e_ready, 1)
        tailed(v_.tensor_reduce(norm[:, 0, :], exp_, AX.X, ALU.add))
        dve.wait_ge(tail, 5)
        tailed(v_.reciprocal(norm[:, 1, :], norm[:, 0, :]))
        dve.wait_ge(tail, 6)
        tailed(v_.tensor_tensor(exp_, exp_, bcast(norm[:, 1, :], TOPK), ALU.mult))
        tile = 4
        for r in range(2):
            for t in range(TT):
                down_low(tile // 2, 0)
                dve.wait_ge(tail, steps[0])
                tailed(v_.tensor_tensor(match[:], bcast(pos_f[:, r, t * SLOTS:(t + 1) * SLOTS], TOPK),
                                        iota[:, 0:TOPK].rearrange("p (a n) -> p a n", a=1).broadcast_to((P, SLOTS, TOPK)),
                                        ALU.is_equal))
                down_low(tile // 2, 1)
                dve.wait_ge(tail, steps[0])
                by_head = match[:].rearrange("p (h k) n -> p h k n", h=HEADS)
                index = si[:, t, :, r:r + 1, :].broadcast_to((P, HEADS, TOPK, TOPK))
                tailed(v_.tensor_tensor(by_head, by_head, index, ALU.mult))
                down_low(tile // 2 + 1, 0)
                dve.wait_ge(tail, steps[0])
                tailed(v_.tensor_reduce(route[:, r, t, :], match[:], AX.X, ALU.add))
                down_low(tile // 2 + 1, 1)
                tile += 4
        assert steps[0] == TAIL_OPS and tile == 20

        def plain(lo, hi):
            with dve.Fori(lo // 2, hi // 2) as it:
                for u in range(2):
                    down_low(it, u)

        def onehots(s, u, half, first=False):
            if not first:
                dve.wait_ge(g_done, s - 1)
            tok = bass.ds((s - (STEPS if half == 0 else 0)) * TOK, TOK)
            first_key, second_key = (slot_key[:, r:r + 1, tok] for r in range(2))
            v_.tensor_tensor(one_i[:, u], iota_tok[:, half * HALF:(half + 1) * HALF, :],
                             first_key.broadcast_to((P, HALF, TOK)), ALU.is_equal).then_inc(eq_ready, 1)
            v_.tensor_tensor(one_j[:, u], iota_tok[:], second_key.broadcast_to((P, P, TOK)), ALU.is_equal).then_inc(eq_ready, 1)
            dve.wait_ge(eq_ready, s * 2 + 2)
            v_.tensor_tensor(gate_i[:, u], one_i[:, u].rearrange("p (a i) t -> p a i t", a=1).broadcast_to((P, PARTS, HALF, TOK)),
                             slot_gate[:, :, tok].rearrange("p r (a t) -> p r a t", a=1).broadcast_to((P, PARTS, HALF, TOK)),
                             ALU.mult).then_inc(onehot_ready, 1)

        def take(s, u, half):
            dve.wait_ge(g_done, s + 1)
            dst = gated[:, half * HALF:(half + 1) * HALF, bass.ds((s - (STEPS if half == 0 else 0)) * TOK, TOK)]
            got = ps[:, 2 + u, 0:TOK * HALF].rearrange("p (t i) -> p i t", t=TOK)
            if half:
                v_.tensor_copy(dst, got).then_inc(g_read, 1)
            else:
                v_.tensor_tensor(dst, dst, got, ALU.mult).then_inc(g_read, 1)

        def meet(i, u):
            dve.wait_ge(gelu_ready, i + 1)
            v_.tensor_tensor(gated_tile(i), gated_tile(i), gelu[:, u, :], ALU.mult).then_inc(tile_ready, 1)

        plain(20, PLAIN_TILES)
        dve.wait_ge(ident_ready, 2)
        dve.wait_ge(slot_ready, 3)
        v_.tensor_tensor(gate_left[:], ps[:, 6, 0:SEQ], slot_gate[:, 0, :], ALU.subtract).then_inc(tail, 1)
        dve.wait_ge(tail, TAIL_OPS + 1)
        v_.tensor_copy(slot_gate[:, 1, :], gate_left[:]).then_inc(tail, 1)
        dve.wait_ge(tail, TAIL_OPS + 2)
        v_.tensor_tensor(slot_gate[:, 2, :], gate_left[:], slot_gate[:, 1, :], ALU.subtract).then_inc(tail, 1)
        dve.wait_ge(tail, TAIL_OPS + 3)
        for i in (PLAIN_TILES, PLAIN_TILES + 1):
            for v in range(2):
                s = 2 * (i - PLAIN_TILES) + v
                down_low(i // 2, i % 2, (2 * v, 2 * v + 1))
                onehots(s, v, 1, first=(s < 2))
                if s >= 2:
                    take(s - 2, v, 1)
        with dve.Fori(PLAIN_TILES // 2 + 1, HALF // 2) as it:
            for u in range(2):
                for v in range(2):
                    s = it * 4 + (2 * u + v - 2 * PLAIN_TILES)
                    down_low(it, u, (2 * v, 2 * v + 1))
                    onehots(s, v, 1)
                    take(s - 2, v, 1)
        for u in range(2):
            down_low(HALF // 2, u)
            onehots(STEPS + u, u, 0)
            take(STEPS - 2 + u, u, 1)
        dve.wait_ge(gelu_ready, HALF)
        dve.wait_ge(g_read, STEPS)
        meet(HALF, 0)
        def low_gated(i, n, u):
            dve.wait_ge(ah_ready, n + 1)
            v_.tensor_tensor(al[u][:], gated_tile(i), ah[:, u, :].bitcast(F32), ALU.subtract).then_inc(al_ready, 1)

        def one_step_tile(it, u):
            down_low(it, u)
            onehots(it * 2 + u, u, 0)
            take(it * 2 + (u - 2), u, 0)
            meet(it * 2 + (u - 1), 1 - u)

        with dve.Fori(HALF // 2 + 1, NKEYS // 2 - 1) as it:
            for u in range(2):
                one_step_tile(it, u)
        for u in range(2):
            one_step_tile(NKEYS // 2 - 1, u)
        low_gated(HALF, 0, 0)
        dve.wait_ge(onehot_ready, 2 * STEPS)
        low_gated(HALF + 1, 1, 1)

        q_up = Q_DOWN + 4 * NKEYS
        low(q_up, 4)
        for u in range(2):
            take(2 * STEPS - 2 + u, u, 0)
        low(q_up + 4, 4)
        meet(NKEYS - 1, 1)
        for lo, hi, shift in ((0, HALF // 2 - 1, HALF), (HALF // 2 - 1, NKEYS // 2 - 1, -HALF)):
            with dve.Fori(lo, hi) as it:
                for u in range(2):
                    low(q_up + 8 + 4 * u, 4, it)
                    low_gated(it * 2 + (u + 2 + shift), it * 2 + (u + 2), u)

        dve.wait_ge(s_res2, 16)
        dve.wait_ge(s_fg, 16)
        def join_experts(t):
            for w in range(4):
                dve.wait_ge(quarter_done, 4 * t + w + 1)
                part = res2[:, t, w * 512:(w + 1) * 512]
                v_.tensor_tensor(part, part, ps[:, 4 * t + w, :], ALU.add).then_inc(h3_ready, 1)

        def last_rstd(t):
            dve.wait_ge(ssq4, 4 * t + 4)
            mean = small[:, 6 + t:7 + t]
            v_.tensor_reduce(mean, small[:, 8 + 4 * t:12 + 4 * t], AX.X, ALU.add).then_inc(sum4, 1)
            dve.wait_ge(sum4, t + 1)
            v_.tensor_scalar(mean, mean, 1.0 / D, RMS_EPS, ALU.mult, ALU.add).then_inc(var4, 1)
            dve.wait_ge(std4, t + 1)
            v_.reciprocal(mean, mean).then_inc(rs4, 1)
            dve.wait_ge(rs4, t + 1)

        def normalise(t, quarters):
            for w in quarters:
                cols = slice(w * 512, (w + 1) * 512)
                v_.scalar_tensor_tensor(out=outb[:, t, cols], in0=res2[:, t, cols], scalar=small[:, 6 + t:7 + t], in1=fg[:, cols],
                                        op0=ALU.mult, op1=ALU.mult).then_inc(fin, 1)

        join_experts(0)
        last_rstd(0)
        normalise(0, (0, 1))
        join_experts(1)
        normalise(0, (2, 3))
        last_rstd(1)
        normalise(1, range(4))

    ctx.close()


def kernel(**inputs):
    import numpy as np
    import concourse.bacc as bacc
    from concourse.bass_utils import run_bass_kernel_spmd

    a = {k: np.asarray(v) for k, v in inputs.items()}

    def columns(v, n):
        return v.reshape(n, P).T

    def stationary(w):
        rows, cols = w.shape
        w = w.reshape(rows // (8 * P), 8, P, cols // P, P).transpose(3, 0, 2, 1, 4)
        return w.reshape(-1, P, CHUNK)

    h = np.concatenate([a["meta_tokens"], a["x"][0]], axis=0)
    w_in = a["w_in"][0]
    conv = w_in[:, W:].reshape(D, 2, CT, P).transpose(0, 2, 1, 3).reshape(D, 2 * W)
    w_in = np.concatenate([conv, w_in[:, :W]], axis=1)
    pool_w = a["pool_w"][0].reshape(2, 2, 2, P, 2, P).transpose(0, 3, 1, 4, 2, 5).reshape(2, P, CHUNK)
    w_out = a["w_out"][0].reshape(2, CT, P, 2, CHUNK)[::-1].transpose(3, 0, 1, 2, 4).reshape(-1, P, CHUNK)
    front = np.concatenate([stationary(w_in), stationary(a["conv_pw_w"][0]), pool_w, w_out, stationary(a["peer_wq"][0])])
    assert front.shape[0] == FRONT
    dw = a["conv_dw_w"][0].reshape(TAPS, CT, P).transpose(2, 1, 0).reshape(P, CT * TAPS)
    vec = np.concatenate([
        columns(a["mix_norm_g"][0], KD), columns(a["pool_scale"][0], CT), dw, columns(a["conv_dw_b"][0], CT),
        columns(a["conv_ln_g"][0], CT), columns(a["conv_ln_b"][0], CT), columns(a["conv_pw_b"][0], CT),
        columns(a["ffn_norm_g"][0], KD)], axis=1)
    up = a["peer_up"][0].reshape(2, HALF, P, 2, CHUNK)[::-1].transpose(0, 1, 3, 2, 4).reshape(2 * NKEYS, P, CHUNK)
    arrays = {
        "hT": h.T.reshape(KD, P, T).transpose(1, 0, 2),
        "x": a["x"][0].reshape(TT, P, D).transpose(1, 0, 2),
        "front": front,
        "down": a["peer_down"][0].reshape(NKEYS, P, 2, 8, P).transpose(0, 2, 4, 3, 1).reshape(2 * NKEYS, P, CHUNK),
        "up": up,
        "keys": a["peer_keys"][0].transpose(3, 0, 1, 2).reshape(P, 2 * HEADS, NKEYS),
        "vec": vec,
        "fg": np.broadcast_to(a["final_norm_g"], (P, D)),
    }
    arrays = {f"in_{k}": np.ascontiguousarray(v) for k, v in arrays.items()}
    nc = bacc.Bacc("TRN2", target_bir_lowering=False, num_devices=1, dynamic_dma_scratch_size=1024)
    aps = [nc.dram_tensor(k, v.shape, mybir.dt.from_np(v.dtype), kind="ExternalInput").ap() for k, v in arrays.items()]
    out = nc.dram_tensor("out", (TT, P, D), F32, kind="ExternalOutput").ap()
    bass_hymba_peer_block(nc, *aps, out)
    r = run_bass_kernel_spmd(nc, [arrays], core_ids=[0])
    return r.results[0]["out"].reshape(1, SEQ, D)
```
